# Optimizing a Trainium2 kernel written in Bass

```python
import jax, jax.numpy as jnp
from jax import lax
import numpy as np

D_MODEL = 1024
BATCH = 1
SEQ = 512
DEPTH = 1

GLA_HEADS = 4
GLA_QK = D_MODEL // 2
GLA_V = D_MODEL
GLA_DK = GLA_QK // GLA_HEADS
GLA_DV = GLA_V // GLA_HEADS
GLA_LOWRANK = 16
GLA_LOGIT_NORM = 16.0
HGRN_EXPAND = 128
HGRN_HEADS = D_MODEL // HGRN_EXPAND
HGRN_K = D_MODEL
HGRN_V = D_MODEL
HGRN_DV = HGRN_V // HGRN_HEADS
D_FF = ((8 * D_MODEL // 3 + 255) // 256) * 256
CONV_W = 3
CHUNK = 64
EPS = 1e-6
IN_SIZES = (GLA_QK, GLA_QK, GLA_V, GLA_V, GLA_LOWRANK,
            HGRN_K, HGRN_K, HGRN_V, HGRN_V, D_MODEL, D_MODEL)
D_IN = sum(IN_SIZES)

kernel_name = "hybrid_gla_hgrn2_convffn_adaln"

def rmsnorm(x, w):
    x32 = x.astype(jnp.float32)
    return x32 * lax.rsqrt(jnp.mean(x32 * x32, axis=-1, keepdims=True) + EPS) * w.astype(jnp.float32)

def chunk_gated_linear_attn(q, k, v, log_g, scale):
    B, T, H, dk = q.shape
    dv = v.shape[-1]
    N = T // CHUNK

    def blk(t):
        return t.astype(jnp.float32).reshape(B, N, CHUNK, H, t.shape[-1]).transpose(0, 3, 1, 2, 4)

    q, k, v, log_g = blk(q) * scale, blk(k), blk(v), blk(log_g)
    b = jnp.cumsum(log_g, axis=3)
    b_ref = b[..., CHUNK // 2 - 1:CHUNK // 2, :]
    b_last = b[..., -1:, :]
    causal = jnp.tril(jnp.ones((CHUNK, CHUNK), dtype=bool))
    scores = jnp.einsum('bhnik,bhnjk->bhnij', q * jnp.exp(b - b_ref), k * jnp.exp(b_ref - b))
    scores = jnp.where(causal, scores, 0.0)
    o_intra = jnp.einsum('bhnij,bhnjv->bhniv', scores, v)
    chunk_state = jnp.einsum('bhnjk,bhnjv->bhnkv', k * jnp.exp(b_last - b), v)
    chunk_decay = jnp.exp(b_last[..., 0, :])

    def step(S, inp):
        d, u = inp
        return d[..., None] * S + u, S

    _, S_prev = lax.scan(step, jnp.zeros((B, H, dk, dv), jnp.float32),
                         (jnp.moveaxis(chunk_decay, 2, 0), jnp.moveaxis(chunk_state, 2, 0)))
    S_prev = jnp.moveaxis(S_prev, 0, 2)
    o_inter = jnp.einsum('bhnik,bhnkv->bhniv', q * jnp.exp(b), S_prev)
    return (o_intra + o_inter).transpose(0, 2, 3, 1, 4).reshape(B, T, H, dv)

def token_mixer(h, w_in, w_gk2, b_gk2, gla_norm_w, lb, hgrn_norm_w, w_out):
    B, T, _ = h.shape
    proj = h @ w_in
    idx = np.cumsum(np.array(IN_SIZES))[:-1].tolist()
    gq, gk, gv, gg, glr, hq, hf, hi, hg, ma, mb = jnp.split(proj, idx, axis=-1)

    def heads(t, n):
        return t.reshape(B, T, n, t.shape[-1] // n)

    log_alpha = jax.nn.log_sigmoid((glr @ w_gk2 + b_gk2).astype(jnp.float32)) / GLA_LOGIT_NORM
    o_a = chunk_gated_linear_attn(heads(gq, GLA_HEADS), heads(gk, GLA_HEADS), heads(gv, GLA_HEADS),
                                  heads(log_alpha, GLA_HEADS), GLA_DK ** -0.5)
    y_a = (rmsnorm(o_a, gla_norm_w) * jax.nn.silu(heads(gg, GLA_HEADS))).reshape(B, T, GLA_V)

    sf = jax.nn.sigmoid(hf.astype(jnp.float32))
    f = lb + (1.0 - lb) * sf
    key = (1.0 - lb) * jax.nn.sigmoid(-hf.astype(jnp.float32))
    o_b = chunk_gated_linear_attn(heads(jax.nn.silu(hq), HGRN_HEADS), heads(key, HGRN_HEADS),
                                  heads(hi, HGRN_HEADS), heads(jnp.log(f), HGRN_HEADS), HGRN_EXPAND ** -0.5)
    y_b = (rmsnorm(o_b, hgrn_norm_w) * jax.nn.silu(heads(hg, HGRN_HEADS))).reshape(B, T, HGRN_V)

    merged = jax.nn.sigmoid(ma) * y_a + jax.nn.sigmoid(mb) * y_b
    return merged @ w_out

def conv_ffn(h, w_up, conv_w, conv_b, w_down):
    u = h @ w_up
    u = lax.conv_general_dilated(u, conv_w[:, None, :].astype(u.dtype), window_strides=(1,),
                                 padding=[(CONV_W - 1, 0)],
                                 dimension_numbers=('NWC', 'WIO', 'NWC'),
                                 feature_group_count=2 * D_FF) + conv_b
    gate, up = jnp.split(u, 2, axis=-1)
    return (jax.nn.silu(gate) * up) @ w_down

def setup_inputs(seed: int = 0) -> dict:
    key = jax.random.key(seed)
    ks = jax.random.split(key, 20)

    def nrm(k, shape, scale):
        return jax.random.normal(k, shape, jnp.float32) * scale

    return {
        "x": nrm(ks[0], (BATCH, SEQ, D_MODEL), 1.0),
        "c": nrm(ks[1], (BATCH, D_MODEL), 1.0),
        "w_ada": nrm(ks[2], (DEPTH, D_MODEL, 6 * D_MODEL), 0.5 * D_MODEL ** -0.5),
        "b_ada": nrm(ks[3], (DEPTH, 6 * D_MODEL), 0.02),
        "norm_mix_w": 1.0 + nrm(ks[4], (DEPTH, D_MODEL), 0.02),
        "w_in": nrm(ks[5], (DEPTH, D_MODEL, D_IN), D_MODEL ** -0.5),
        "w_gk2": nrm(ks[6], (DEPTH, GLA_LOWRANK, GLA_QK), GLA_LOWRANK ** -0.5),
        "b_gk2": nrm(ks[7], (DEPTH, GLA_QK), 0.1),
        "gla_norm_w": 1.0 + nrm(ks[8], (DEPTH, GLA_DV), 0.02),
        "hgrn_lb": nrm(ks[9], (DEPTH + 1, HGRN_K), 0.1),
        "hgrn_norm_w": 1.0 + nrm(ks[10], (DEPTH, HGRN_DV), 0.02),
        "w_out": nrm(ks[11], (DEPTH, D_MODEL, D_MODEL), D_MODEL ** -0.5),
        "norm_ffn_w": 1.0 + nrm(ks[12], (DEPTH, D_MODEL), 0.02),
        "w_up": nrm(ks[13], (DEPTH, D_MODEL, 2 * D_FF), D_MODEL ** -0.5),
        "conv_w": nrm(ks[14], (DEPTH, CONV_W, 2 * D_FF), CONV_W ** -0.5),
        "conv_b": nrm(ks[15], (DEPTH, 2 * D_FF), 0.02),
        "w_down": nrm(ks[16], (DEPTH, D_FF, D_MODEL), D_FF ** -0.5),
        "final_norm_w": 1.0 + nrm(ks[17], (D_MODEL,), 0.02),
    }

def reference(x, c, w_ada, b_ada, norm_mix_w, w_in, w_gk2, b_gk2, gla_norm_w, hgrn_lb,
              hgrn_norm_w, w_out, norm_ffn_w, w_up, conv_w, conv_b, w_down, final_norm_w):
    out_dtype = x.dtype
    lb_all = jnp.cumsum(jax.nn.softmax(hgrn_lb.astype(jnp.float32), axis=0), axis=0)
    c_act = jax.nn.silu(c.astype(jnp.float32))
    h_res = x
    for l in range(DEPTH):
        ada = c_act @ w_ada[l] + b_ada[l]
        sh_a, sc_a, g_a, sh_f, sc_f, g_f = [t[:, None, :] for t in jnp.split(ada, 6, axis=-1)]
        h = rmsnorm(h_res, norm_mix_w[l]) * (1.0 + sc_a) + sh_a
        h_res = h_res + g_a * token_mixer(h, w_in[l], w_gk2[l], b_gk2[l], gla_norm_w[l],
                                          lb_all[l], hgrn_norm_w[l], w_out[l])
        h = rmsnorm(h_res, norm_ffn_w[l]) * (1.0 + sc_f) + sh_f
        h_res = h_res + g_f * conv_ffn(h, w_up[l], conv_w[l], conv_b[l], w_down[l])
    return rmsnorm(h_res, final_norm_w).astype(out_dtype)


_drawn_inputs = setup_inputs


def setup_inputs(seed=0):
    import zlib

    import numpy as np

    out = dict(_drawn_inputs(seed))
    spreads = {}
    factors = {'b_ada': 2.736,
     'norm_mix_w': 8.0,
     'w_gk2': 2.728,
     'b_gk2': 8.0,
     'gla_norm_w': 27.145,
     'hgrn_lb': 8.0,
     'hgrn_norm_w': 22.985,
     'norm_ffn_w': 22.748,
     'conv_b': 21.99,
     'final_norm_w': 8.503}
    for name, (base, spread) in spreads.items():
        noise = np.random.default_rng([zlib.crc32(name.encode()), seed]).standard_normal(out[name].shape)
        drawn = base * np.exp(spread * noise) if base else spread * noise
        out[name] = __import__('jax').numpy.asarray(drawn.astype(out[name].dtype))
    for name, factor in factors.items():
        out[name] = (out[name] * factor).astype(out[name].dtype)
    return out
```

```python
from contextlib import ExitStack

import concourse.bass as bass
from concourse import mybir

F32 = mybir.dt.float32
F32R = mybir.dt.float32r
BF16 = mybir.dt.bfloat16
U32 = mybir.dt.uint32
ALU = mybir.AluOpType
ACT = mybir.ActivationFunctionType

P = 128
D = 1024
T = 512
KT = D // P
TT = T // P
CHUNK = 64
NCH = T // CHUNK
GROUPS = 4
D_FF = 2816
FT = D_FF // P
GLA_QK, GLA_V, LOWRANK = 512, 1024, 16
GLA_DV = GLA_V // GROUPS
HGRN_DV = 128
LOGIT_NORM = 16.0
SCALE2 = 1.0 / 128
EPS = 1e-6

GQ, GK, GV, GG = 0, GLA_QK, 2 * GLA_QK, 2 * GLA_QK + GLA_V
GLR = GG + GLA_V
HQ = GLR + LOWRANK
HF, HI, HG, MA, MB = (HQ + i * D for i in range(1, 6))
UNITS = [(GV, 256), (GV + P, 256), (HI, 256), (HI + P, 256), (GQ, P), (GK, P),
         (HF, 256), (HF + P, 256), (HQ, 256), (HQ + P, 256),
         (GG, 256), (MA, 256), (GG + P, 256), (MA + P, 256),
         (HG, 256), (MB, 256), (HG + P, 256), (MB + P, 256)]
NU = len(UNITS)
U_MIX = 1
U_OUT = U_MIX + GROUPS * NU
U_UP = U_OUT + KT
U_DOWN = U_UP + 2 * FT
U_END = U_DOWN + FT
RING, RAW = 6, 3
AHEAD = 4
BY_DVE = (8, 9, 10, 12, 14, 16)

B_PROJ, B_MISC, B_STATE, B_O = 0, 2, 4, 6
MISC_Z = 2
MISC_T = (2, 3, 2)
MISC_S = (3, 2, 3)
MISC_SS = (3, 2, 3)

V_BADA, V_NMIX, V_NFFN, V_CONVB, V_LB, V_BGK = 0, 48, 56, 64, 108, 124
V_TAP0, V_TAP1, V_C, V_GNW, V_HNW, V_TAP2 = 128, 172, 216, 224, 226, 256


def slot(u):
    return (u + 5) % RING


def raw_slot(u):
    return (u + 2) % RAW


def raw_count(u):
    return u // RAW + 1


def taken_counts(n):
    if n in BY_DVE:
        return True, BY_DVE.index(n) + 1
    return False, len([m for m in range(n + 1) if m not in BY_DVE])


N_DVE = len(BY_DVE)
N_ACT = NU - N_DVE


def build(nc, x, c, w_ada, b_ada, norm_mix_w, w_in, w_gk2, b_gk2, gla_norm_w, hgrn_lb, hgrn_norm_w,
          w_out, norm_ffn_w, w_up, conv_w, conv_b, w_down, final_norm_w, out):
    ctx = ExitStack()
    with ctx:
        def sem(name):
            return ctx.enter_context(nc.semaphore(name))

        def sbuf(stack):
            def alloc(name, shape, dt=F32):
                return stack.enter_context(nc.sbuf_tensor(name, shape, dt))
            return alloc

        sb = sbuf(ctx)
        raw = sb("raw", [P, RAW, KT, P])
        w_hi = sb("w_hi", [P, RING, KT, P], F32R)
        w_lo = sb("w_lo", [P, RING, KT, P], F32R)
        h_hi = sb("h_hi", [P, KT, T], F32R)
        h_lo = sb("h_lo", [P, KT, T], F32R)
        vecs = sb("vecs", [P, 3 * P])
        ada = sb("ada", [P, 48])
        ident = sb("ident", [P, P])
        ones = sb("ones", [P, P])
        cols = sb("cols", [P, 64])
        eps_c, one_c = cols[:, 0:1], cols[:, 1:2]
        c_act = cols[:, 2:10]
        a_mix = cols[:, 10:18]
        lb, omlb = cols[:, 18:26], cols[:, 26:34]
        a_ffn = cols[:, 34:42]
        gnw, hnw = cols[:, 42:44], cols[:, 44:45]
        ssq, rst = cols[:, 45:49], cols[:, 49:53]
        qscale = cols[:, 53:54]
        fss, frs = cols[:, 54:58], cols[:, 58:62]

        init = ExitStack()
        si = sbuf(init)
        rows = si("rows", [P, 3, P])
        x_tok = si("x_tok", [P, TT, D])
        xn_tok = si("xn_tok", [P, TT, D])
        xnT = si("xnT", [P, KT, T])
        xT = si("xT", [P, KT, T])
        ada_w0 = si("ada_w0", [P, 4, KT, 256])
        h_tmp = si("h_tmp", [P, 2, T])
        lbt = si("lbt", [P, 5, KT])
        init.close()

        mix = ExitStack()
        sm = sbuf(mix)
        merged = sm("merged", [P, KT, T])
        ada_w = sm("ada_w", [P, 2, KT, P])
        v = sm("v", [P, TT, 4 * P])
        qs = sm("qs", [P, 2, T])
        ks = sm("ks", [P, 2, T])
        qe = sm("qe", [P, 2, T])
        kp = sm("kp", [P, 2, T])
        bcum = sm("bcum", [P, 2, T])
        d_ref = sm("d_ref", [P, 2, T])
        d_last = sm("d_last", [P, 2, T])
        lg = sm("lg", [P, 2, T])
        key = sm("key", [P, 2, T])
        qry = sm("qry", [P, 2, T])
        decay = sm("decay", [P, 3, NCH])
        kT = sm("kT", [P, TT, P])
        sT = sm("sT", [P, TT, P])
        state = sm("state", [P, NCH - 1, P])
        gate = sm("gate", [P, 4, T])
        gmul = sm("gmul", [P, T])
        sq = sm("sq", [P, 2, T])
        oe = sm("oe", [P, 2, T])
        rn = sm("rn", [P, T])
        lrT = sm("lrT", [LOWRANK, T])
        gk2 = sm("gk2", [32 + LOWRANK, T])
        scan_mask = sm("scan_mask", [P, T], BF16)
        causal = sm("causal", [P, P])
        mix.close()

        sf = sbuf(ctx)
        prod = sf("prod", [P, FT, T])
        hres = sf("hres", [P, KT, T])
        hres_tok = sf("hres_tok", [P, TT, D])
        conv = sf("conv", [P, 6, T])
        n_tmp = sf("n_tmp", [P, 2, T])
        rn2 = sf("rn2", [P, T])
        fw_b = sf("fw_b", [P, D])
        gf_b = sf("gf_b", [P, D])
        xT_dram = nc.dram_tensor("xT_saved_dram", [P, KT, T], F32, kind="Internal").ap()

        ps = ctx.enter_context(nc.psum_tensor("ps", [P, 8, T], F32))

        rows_zero = sem("rows_zero")
        rows_in = sem("rows_in")
        x_in = sem("x_in")
        gk2_in = sem("gk2_in")
        fw_in = sem("fw_in")
        ada0_in = [sem(f"ada0_in{i}") for i in range(4)]
        ada_in = [sem(f"ada_in{i}") for i in range(2)]
        raw_in = [sem(f"raw_in{i}") for i in range(RAW)]
        xT_out = sem("xT_out")
        xT_back = sem("xT_back")
        out_done = sem("out_done")
        const_made = sem("const_made")
        cols_made = sem("cols_made")
        mask_made = sem("mask_made")
        vecs_turned = sem("vecs_turned")
        vecs_made = sem("vecs_made")
        start_act = sem("start_act")
        start_dve = sem("start_dve")
        x_turned = sem("x_turned")
        xT_made = sem("xT_made")
        xnT_made = sem("xnT_made")
        ada0_used = sem("ada0_used")
        ada0_made = sem("ada0_made")
        h_tmp_made = sem("h_tmp_made")
        h_hi_made = sem("h_hi_made")
        h_lo_made = sem("h_lo_made")
        hi_made = sem("hi_made")
        lo_made = sem("lo_made")
        proj_done = sem("proj_done")
        taken_act = sem("taken_act")
        taken_dve = sem("taken_dve")
        ada_used = sem("ada_used")
        ada_made = sem("ada_made")
        gk2_made = sem("gk2_made")
        z_done = sem("z_done")
        z_made = sem("z_made")
        soft_step = sem("soft_step")
        ln_made = sem("ln_made")
        sig_made = sem("sig_made")
        la_made = sem("la_made")
        scan_made = sem("scan_made")
        d_made = sem("d_made")
        exp_made = sem("exp_made")
        kk_made = sem("kk_made")
        qq_made = sem("qq_made")
        turned = sem("turned")
        kT_made = sem("kT_made")
        scored = sem("scored")
        sT_made = sem("sT_made")
        u_done = sem("u_done")
        state_made = sem("state_made")
        o_done = sem("o_done")
        o_taken = sem("o_taken")
        sq_made = sem("sq_made")
        ss_done = sem("ss_done")
        ss_taken = sem("ss_taken")
        rn_made = sem("rn_made")
        normed = sem("normed")
        gated = sem("gated")
        y_made = sem("y_made")
        merged_made = sem("merged_made")
        m_hi_made = sem("m_hi_made")
        m_lo_made = sem("m_lo_made")
        hres_made = sem("hres_made")
        sq2_made = sem("sq2_made")
        ss2_step = sem("ss2_step")
        rn2_step = sem("rn2_step")
        a_ffn_made = sem("a_ffn_made")
        n_made = sem("n_made")
        n_hi_made = sem("n_hi_made")
        n_lo_made = sem("n_lo_made")
        diag_made = sem("diag_made")
        gf_done = sem("gf_done")
        gf_made = sem("gf_made")
        ht_done = sem("ht_done")
        ht_made = sem("ht_made")
        conv_a = sem("conv_a")
        conv_b_ = sem("conv_b_")
        conv_made = sem("conv_made")
        gate_made = sem("gate_made")
        prod_made = sem("prod_made")
        p_hi_made = sem("p_hi_made")
        p_lo_made = sem("p_lo_made")
        y_done = sem("y_done")
        fin_step = sem("fin_step")
        fsq_made = sem("fsq_made")
        frs_made = sem("frs_made")
        fin_made = sem("fin_made")

        def unit_view(w):
            return w[0].rearrange("(k p) c -> p k c", p=P)

        win_v, wout_v, wup_v, wada_v = map(unit_view, (w_in, w_out, w_up, w_ada))
        wdown_v = w_down[0].rearrange("(f p) n -> f p n", p=P)

        def prod_wait(eng, g, n):
            m = n - 2
            gg = g
            if m < 0:
                m, gg = m + NU, g - 1
            dve, k = taken_counts(m)
            if dve:
                eng.wait_ge(taken_dve, gg * N_DVE + k)
            else:
                eng.wait_ge(taken_act, gg * N_ACT + k + 1)

        block = ctx.enter_context(nc.Block())

        @block.sync
        def _(sp):
            sp.wait_ge(rows_zero, 1)
            def row(dst, src, n):
                sp.dma_start(rows[dst % P:dst % P + n, dst // P, :], src).then_inc(rows_in, 16)
            row(V_C, c[0].rearrange("(r p) -> r p", p=P), 8)
            row(V_BADA, b_ada[0].rearrange("(r p) -> r p", p=P), 48)
            row(V_NMIX, norm_mix_w[0].rearrange("(r p) -> r p", p=P), 8)
            row(V_NFFN, norm_ffn_w[0].rearrange("(r p) -> r p", p=P), 8)
            row(V_CONVB, conv_b[0].rearrange("(r p) -> r p", p=P), 44)
            row(V_LB, hgrn_lb.rearrange("a (r p) -> (a r) p", p=P), 16)
            row(V_BGK, b_gk2[0].rearrange("(r p) -> r p", p=P), 4)
            row(V_TAP0, conv_w[0, 0:2].rearrange("a (r p) -> (a r) p", p=P), 88)
            row(V_GNW, gla_norm_w[0].rearrange("(r p) -> r p", p=P), 2)
            row(V_HNW, hgrn_norm_w[0].rearrange("(r p) -> r p", p=P), 1)
            row(V_TAP2, conv_w[0, 2].rearrange("(r p) -> r p", p=P), 44)
            for i in range(8):
                if i >= 4:
                    sp.wait_ge(ada0_used, i - 3)
                sp.dma_start(ada_w0[:, i % 4], wada_v[:, :, i * 256:(i + 1) * 256]).then_inc(ada0_in[i % 4], 16)
            sp.dma_start(raw[:, raw_slot(0)], win_v[:, :, GLR:GLR + P]).then_inc(raw_in[raw_slot(0)], 16)
            sp.wait_ge(xT_made, KT)
            sp.dma_start(xT_dram, xT[:]).then_inc(xT_out, 16)

            def load(u, src, free):
                if free is not None:
                    sp.wait_ge(lo_made, free)
                sp.dma_start(raw[:, raw_slot(u)], src).then_inc(raw_in[raw_slot(u)], 16)

            def group_loads(g, first):
                for n in range(NU):
                    c0, step = UNITS[n]
                    u = U_MIX + n
                    load(u, win_v[:, :, bass.ds(g * step + c0, P)],
                         None if first and u < RAW else g * NU + u - RAW + 1)
                    if 5 <= n < 13:
                        m = n - 5
                        if not (first and m < 2):
                            sp.wait_ge(ada_used, g * 8 + m - 1)
                        elif m == 0:
                            sp.wait_ge(xT_out, 16)
                            sp.wait_ge(proj_done, 1)
                        sp.dma_start(ada_w[:, m % 2], wada_v[:, :, bass.ds(g * D + 2 * D + m * P, P)]
                                     ).then_inc(ada_in[m % 2], 16)

            group_loads(0, True)
            with sp.Fori(1, GROUPS) as g:
                group_loads(g, False)
            for j in range(KT):
                load(U_OUT + j, wout_v[:, :, j * P:(j + 1) * P], U_OUT + j - RAW + 1)
                if j == 3:
                    sp.wait_ge(m_lo_made, KT)
                    sp.dma_start(hres[:], xT_dram).then_inc(xT_back, 16)
                    sp.dma_start(fw_b[:], final_norm_w.rearrange("(a d) -> a d", a=1).to_broadcast([P, D])
                                 ).then_inc(fw_in, 16)
            with sp.Fori(0, 7) as r:
                for m in range(6):
                    u = U_UP + m
                    load(u, wup_v[:, :, bass.ds(r * 3 * P + (m // 2) * P + (m % 2) * D_FF, P)],
                         r * 6 + u - RAW + 1)
            for m in range(2):
                u = U_UP + 42 + m
                load(u, wup_v[:, :, 21 * P + m * D_FF:22 * P + m * D_FF], u - RAW + 1)
            with sp.Fori(0, 3) as r:
                for m in range(6):
                    u = U_DOWN + m
                    load(u, wdown_v[bass.ds(r * 6 + m, 1)].rearrange("a p n -> (a p) n"), r * 6 + u - RAW + 1)
            for f in range(18, FT):
                u = U_DOWN + f
                load(u, wdown_v[f], u - RAW + 1)
            for t in range(TT):
                sp.wait_ge(fin_made, t + 1)
                sp.dma_start(out[0, t * P:(t + 1) * P, :], hres_tok[:, t, :]).then_inc(out_done, 16)
            sp.wait_ge(out_done, 16 * TT)

        @block.gpsimd
        def _(pool):
            pool.memset(ones[:], 1.0).then_inc(const_made, 1)
            pool.memset(ident[:], 0.0).then_inc(const_made, 1)
            pool.wait_ge(const_made, 2)
            pool.affine_select(out=ident[:], in_=ident[:], compare_op=ALU.not_equal, fill=1.0, base=0,
                               pattern=[[-1, P]], channel_multiplier=1).then_inc(const_made, 1)
            pool.wait_ge(xT_out, 16)
            pool.wait_ge(proj_done, 1)
            pool.dma_start(gk2[32:32 + LOWRANK, :], w_gk2[0]).then_inc(gk2_in, 16)
            pool.memset(scan_mask[:], 1.0).then_inc(mask_made, 1)
            pool.memset(causal[:], 1.0).then_inc(mask_made, 1)
            pool.wait_ge(mask_made, 2)
            pool.memset(scan_mask[:].rearrange("p (c t) -> p c t", t=CHUNK)[:, :, 0:1], 0.0).then_inc(mask_made, 1)
            pool.affine_select(out=causal[:], in_=causal[:], compare_op=ALU.is_ge, fill=0.0, base=0,
                               pattern=[[1, P]], channel_multiplier=-1).then_inc(mask_made, 1)
            pool.wait_ge(mask_made, 4)
            pool.memset(causal[0:CHUNK, CHUNK:P], 0.0).then_inc(mask_made, 1)
            pool.memset(sT[:], 0.0).then_inc(mask_made, 1)
            def times_q(g, h, q):
                s = h % 2
                pool.wait_ge(exp_made, g * 15 + 5 * h + 4)
                pool.tensor_tensor(qs[:, s], qs[:, s], q, ALU.mult).then_inc(qq_made, 1)
                pool.wait_ge(exp_made, g * 15 + 5 * h + 5)
                pool.tensor_tensor(qe[:, s], qe[:, s], q, ALU.mult).then_inc(qq_made, 1)

            def gate_mul(g, w):
                pool.wait_ge(taken_dve, g * N_DVE + taken_counts(10 + 2 * w)[1])
                pool.wait_ge(taken_act, g * N_ACT + taken_counts(11 + 2 * w)[1] + 1)
                pool.tensor_tensor(gate[:, w], gate[:, w], gmul[:], ALU.mult).then_inc(gated, 1)

            def gated_y(g, w):
                pool.wait_ge(gated, g * 4 + w + 1)
                pool.wait_ge(normed, g * 4 + w + 1)
                pool.tensor_tensor(gate[:, w], gate[:, w], oe[:, w % 2], ALU.mult).then_inc(y_made, 1)

            def merge(g, w):
                pool.wait_ge(y_made, g * 4 + w + 1)
                pool.tensor_tensor(merged[:, bass.ds(g * 2 + (w - 2), 1), :].rearrange("p a t -> p (a t)"),
                                   gate[:, w - 2], gate[:, w], ALU.add).then_inc(merged_made, 1)

            with pool.Fori(0, GROUPS) as g:
                pool.wait_ge(taken_act, g * N_ACT + taken_counts(5)[1] + 1)
                times_q(g, 0, qry[:, 1])
                pool.wait_ge(taken_dve, g * N_DVE + 1)
                times_q(g, 1, qry[:, 0])
                pool.wait_ge(taken_dve, g * N_DVE + 2)
                times_q(g, 2, qry[:, 1])
                gate_mul(g, 0)
                gate_mul(g, 1)
                gated_y(g, 0)
                gated_y(g, 1)
                gate_mul(g, 2)
                gated_y(g, 2)
                merge(g, 2)
                gate_mul(g, 3)
                gated_y(g, 3)
                merge(g, 3)

            with pool.Fori(0, 7) as r:
                for q in range(3):
                    pool.wait_ge(gate_made, r * 3 + q + 1)
                    pool.wait_ge(conv_made, r * 6 + 2 * q + 2)
                    pool.tensor_tensor(prod[:, bass.ds(r * 3 + q, 1), :].rearrange("p a t -> p (a t)"),
                                       conv[:, 2 * q], conv[:, 2 * q + 1], ALU.mult).then_inc(prod_made, 1)
            pool.wait_ge(gate_made, 22)
            pool.wait_ge(conv_made, 44)
            pool.tensor_tensor(prod[:, 21], conv[:, 0], conv[:, 1], ALU.mult).then_inc(prod_made, 1)

        @block.scalar
        def _(act):
            def split_hi(u, count, free):
                act.wait_ge(raw_in[raw_slot(u)], count)
                if free is not None:
                    act.wait_ge(proj_done, free)
                act.activation(w_hi[:, slot(u)].rearrange("p k c -> p (k c)"),
                               raw[:, raw_slot(u)].rearrange("p k c -> p (k c)"), ACT.Copy).then_inc(hi_made, 1)

            def split_hi_g(g, n):
                u = U_MIX + n
                free = u - 5
                if 6 <= n < 10:
                    free = U_MIX + 4
                split_hi(u, (g * (NU // RAW) + raw_count(u)) * 16, g * NU + free)

            act.dma_start(x_tok[:], x[0].rearrange("(t p) d -> p t d", p=P)).then_inc(x_in, 16)
            act.wait_ge(x_in, 16)
            for t in range(TT):
                act.activation(xn_tok[:, t], x_tok[:, t], ACT.Square, accum_out=ssq[:, t:t + 1]).then_inc(start_act, 1)
            act.wait_ge(start_dve, 2)
            act.activation(rst[:, :], rst[:, :], ACT.Sqrt).then_inc(start_act, 1)
            act.wait_ge(start_act, 5)
            for t in range(TT):
                act.activation(xn_tok[:, t], x_tok[:, t], ACT.Copy, scale=rst[:, t:t + 1]).then_inc(start_act, 1)
            act.wait_ge(vecs_made, 3)
            act.activation(c_act, vecs[:, V_C:V_C + 8], ACT.Sigmoid).then_inc(start_act, 1)
            act.wait_ge(start_dve, 5)
            act.activation(lbt[:, 1:3].rearrange("p a k -> p (a k)"), lbt[:, 1:3].rearrange("p a k -> p (a k)"),
                           ACT.Exp).then_inc(start_act, 1)
            for k in range(KT):
                act.wait_ge(x_turned, 2 * k + 2)
                act.activation(xnT[:, k], ps[:, 2 * (k % 2) + 3], ACT.Copy).then_inc(xnT_made, 1)
            split_hi(0, 16, None)
            act.wait_ge(ada0_made, 2)
            for k in range(KT):
                act.wait_ge(xnT_made, k + 1)
                act.activation(h_hi[:, k], xnT[:, k], ACT.Identity, bias=ada[:, k:k + 1],
                               scale=a_mix[:, k:k + 1]).then_inc(h_hi_made, 1)
            for n in range(AHEAD):
                split_hi(U_MIX + n, 16 * raw_count(U_MIX + n), None)
            act.wait_ge(proj_done, 1)
            act.wait_ge(xT_out, 16)
            act.activation(lrT[:, :], ps[0:LOWRANK, B_PROJ], ACT.Copy).then_inc(taken_act, 1)

            def exps(g, h, inv):
                s = h % 2
                act.wait_ge(d_made, g * 6 + 2 * h + 2)
                if h == 2:
                    act.wait_ge(o_done, g * 4 + 2)
                act.activation(kp[:, s], d_last[:, s], ACT.Exp, scale=-inv).then_inc(exp_made, 1)
                act.activation(decay[:, h], bcum[:, s, CHUNK - 1::CHUNK], ACT.Exp, scale=inv).then_inc(exp_made, 1)
                act.activation(ks[:, s], d_ref[:, s], ACT.Exp, scale=-inv).then_inc(exp_made, 1)
                act.activation(qs[:, s], d_ref[:, s], ACT.Exp, scale=inv).then_inc(exp_made, 1)
                act.activation(qe[:, s], bcum[:, s], ACT.Exp, scale=inv).then_inc(exp_made, 1)

            def take_kT(g, h, u_free):
                act.wait_ge(turned, g * 3 + h + 1)
                act.wait_ge(u_done, g * 4 + u_free)
                act.activation(kT[:].rearrange("p t c -> p (t c)"), ps[:, MISC_T[h]], ACT.Copy).then_inc(kT_made, 1)

            def take_o(g, w, nw):
                act.wait_ge(o_done, g * 4 + w + 1)
                act.wait_ge(y_made, g * 4 + max(w - 1, 0))
                act.wait_ge(ss_done, g * 3 + w // 2)
                act.activation(sq[:, w % 2], ps[:, B_O + w % 2], ACT.Square).then_inc(sq_made, 1)
                act.activation(oe[:, w % 2], ps[:, B_O + w % 2], ACT.Copy, scale=nw).then_inc(o_taken, 1)

            def root(g, i, bank, dv):
                act.wait_ge(ss_done, g * 3 + i + 1)
                act.wait_ge(normed, g * 4 + (0, 2, 3)[i])
                act.activation(rn[:], ps[:, bank], ACT.Ln, bias=eps_c, scale=SCALE2 / dv).then_inc(ss_taken, 1)
                act.wait_ge(ss_taken, g * 3 + i + 1)
                act.activation(rn[:], rn[:], ACT.Exp, scale=-0.5).then_inc(rn_made, 1)

            with act.Fori(0, GROUPS) as g:
                for n in range(NU):
                    if n in (0, 1) or n >= 5:
                        split_hi_g(g, n + AHEAD)
                    if n == 4:
                        for m in (6, 7, 8):
                            split_hi_g(g, m)
                    if n == 10:
                        exps(g, 1, 1.0)
                    if n == 11:
                        exps(g, 2, 1.0)
                    act.wait_ge(proj_done, g * NU + n + 2)
                    bank = ps[:, B_PROJ + (U_MIX + n) % 2]
                    if n < 4:
                        act.activation(v[:, n], bank, ACT.Copy).then_inc(taken_act, 1)
                    if n == 4:
                        act.wait_ge(qq_made, g * 6)
                        act.activation(qry[:, 1], bank, ACT.Copy).then_inc(taken_act, 1)
                    if n == 5:
                        act.activation(key[:, 1], bank, ACT.Copy).then_inc(taken_act, 1)
                    if n in (6, 7):
                        i = n - 6
                        if i == 0:
                            act.wait_ge(la_made, g + 1)
                            act.wait_ge(scan_made, g * 3 + 1)
                        else:
                            act.wait_ge(kk_made, g * 6 + 2)
                        act.activation(lg[:, i], bank, ACT.Sigmoid).then_inc(sig_made, 1)
                        act.activation(key[:, i], bank, ACT.Sigmoid, scale=-1.0).then_inc(taken_act, 1)
                    if n in (8, 9):
                        i = n - 8
                        act.wait_ge(qq_made, g * 6 + 2)
                        act.activation(qry[:, i], bank, ACT.Sigmoid).then_inc(sig_made, 1)
                    if n in (10, 12, 14, 16):
                        w = (n - 10) // 2
                        act.wait_ge(merged_made, g * 2)
                        act.activation(gate[:, w], bank, ACT.Sigmoid).then_inc(sig_made, 1)
                    if n in (11, 13, 15, 17):
                        w = (n - 11) // 2
                        act.wait_ge(gated, g * 4 + w)
                        act.activation(gmul[:], bank, ACT.Sigmoid).then_inc(taken_act, 1)
                    if n == 3:
                        act.wait_ge(z_made, g + 1)
                        act.activation(lg[:, 1], lg[:, 0], ACT.Abs).then_inc(soft_step, 1)
                        act.wait_ge(soft_step, g * 3 + 1)
                        act.activation(lg[:, 1], lg[:, 1], ACT.Exp, scale=-1.0).then_inc(soft_step, 1)
                        act.wait_ge(soft_step, g * 3 + 2)
                        act.activation(lg[:, 1], lg[:, 1], ACT.Ln, bias=one_c).then_inc(soft_step, 1)
                    if n == 5:
                        exps(g, 0, 1.0 / LOGIT_NORM)
                    if n == 8:
                        take_kT(g, 0, 0)
                    if n == 9:
                        for i in range(2):
                            act.wait_ge(sig_made, g * 8 + i + 1)
                            act.activation(lg[:, i], lg[:, i], ACT.Ln, bias=lb[:, bass.ds(g * 2 + i, 1)],
                                           scale=omlb[:, bass.ds(g * 2 + i, 1)]).then_inc(ln_made, 1)
                    if n == 10:
                        take_o(g, 0, gnw[:, 0:1])
                    if n == 11:
                        take_o(g, 1, gnw[:, 1:2])
                    if n == 12:
                        take_kT(g, 1, 2)
                        root(g, 0, MISC_SS[0], GLA_DV)
                    if n == 14:
                        take_kT(g, 2, 3)
                        take_o(g, 2, hnw)
                    if n == 16:
                        take_o(g, 3, hnw)
                        root(g, 1, MISC_SS[1], HGRN_DV)
                    if n == 17:
                        root(g, 2, MISC_SS[2], HGRN_DV)

            act.wait_ge(proj_done, U_OUT)
            for k in range(KT):
                act.wait_ge(merged_made, k + 1)
                act.activation(h_hi[:, k], merged[:, k], ACT.Copy).then_inc(m_hi_made, 1)
            for j in range(KT):
                u = U_OUT + j + AHEAD
                split_hi(u, 16 * raw_count(u), u - 5)
                act.wait_ge(hres_made, j + 1)
                if j >= 2:
                    act.wait_ge(ss2_step, j - 1)
                act.activation(n_tmp[:, j % 2], hres[:, j], ACT.Square).then_inc(sq2_made, 1)
            act.wait_ge(ss2_step, KT)
            act.activation(rn2[:], ps[:, B_MISC], ACT.Ln, bias=eps_c, scale=1.0 / D).then_inc(rn2_step, 1)
            act.wait_ge(rn2_step, 1)
            act.activation(rn2[:], rn2[:], ACT.Exp, scale=-0.5).then_inc(rn2_step, 1)
            act.wait_ge(a_ffn_made, 1)
            for k in range(KT):
                act.wait_ge(n_made, k + 1)
                act.activation(h_hi[:, k], n_tmp[:, k % 2], ACT.Identity, bias=ada[:, 24 + k:25 + k],
                               scale=a_ffn[:, k:k + 1]).then_inc(n_hi_made, 1)
            act.wait_ge(gf_done, 1)
            act.activation(gf_b[:].rearrange("p (a b) -> p a b", a=2), ps[:, B_O:B_O + 2], ACT.Copy).then_inc(gf_made, 1)

            def conv_unit(r, m):
                u = U_UP + m
                split_hi(u + AHEAD, (r * 2 + raw_count(u + AHEAD)) * 16, r * 6 + u + AHEAD - 5)
                ch = r * 3 + (m // 2) + (m % 2) * FT
                act.wait_ge(proj_done, r * 6 + u + 1)
                act.activation(conv[:, m], ps[:, m], ACT.Identity, bias=vecs[:, bass.ds(ch + V_CONVB, 1)],
                               scale=vecs[:, bass.ds(ch + V_TAP2, 1)]).then_inc(conv_a, 1)

            def silu_unit(r, m):
                act.wait_ge(conv_made, r * 6 + m + 1)
                act.activation(conv[:, m], conv[:, m], ACT.Silu).then_inc(gate_made, 1)

            for m in range(6):
                conv_unit(0, m)
                if m < TT:
                    act.wait_ge(ht_done, m + 1)
                    act.activation(hres_tok[:, m].rearrange("p (a b) -> p a b", a=2), ps[:, B_O:B_O + 2],
                                   ACT.Copy).then_inc(ht_made, 1)
                if m % 2:
                    silu_unit(0, m - 1)
            with act.Fori(1, 7) as r:
                for m in range(6):
                    act.wait_ge(prod_made, r * 3 + m // 2 - 2)
                    conv_unit(r, m)
                    if m % 2:
                        silu_unit(r, m - 1)
            act.wait_ge(prod_made, 19)
            for m in range(2):
                u = U_UP + 42 + m
                split_hi(u + AHEAD, 16 * raw_count(u + AHEAD), u + AHEAD - 5)
                act.wait_ge(proj_done, u + 1)
                ch = 21 + m * FT
                act.activation(conv[:, m], ps[:, m], ACT.Identity, bias=vecs[:, V_CONVB + ch:V_CONVB + ch + 1],
                               scale=vecs[:, V_TAP2 + ch:V_TAP2 + ch + 1]).then_inc(conv_a, 1)
            act.wait_ge(conv_made, 43)
            act.activation(conv[:, 0], conv[:, 0], ACT.Silu).then_inc(gate_made, 1)

            def prod_hi(r, f, free):
                act.wait_ge(prod_made, r * 6 + f + 1)
                act.wait_ge(proj_done, free)
                act.activation(h_hi[:, f % 6], prod[:, bass.ds(r * 6 + f, 1), :].rearrange("p a t -> p (a t)"),
                               ACT.Copy).then_inc(p_hi_made, 1)

            for f in range(AHEAD):
                prod_hi(0, f, U_DOWN)
            with act.Fori(0, 3) as r:
                for m in range(6):
                    u = U_DOWN + m + AHEAD
                    split_hi(u, (r * 2 + raw_count(u)) * 16, r * 6 + u - 5)
                    prod_hi(r, m + AHEAD, r * 6 + max(u - 5, U_DOWN))
            for t in range(TT):
                act.wait_ge(fin_step, 2 * t + 2)
                act.activation(prod[:, 0:2].rearrange("p a t -> p (a t)"), hres_tok[:, t], ACT.Square,
                               accum_out=fss[:, t:t + 1]).then_inc(fsq_made, 1)
                act.wait_ge(frs_made, 2 * t + 2)
                act.activation(frs[:, t:t + 1], frs[:, t:t + 1], ACT.Sqrt).then_inc(fsq_made, 1)

        @block.vector
        def _(dve):
            def split_lo(u, count):
                dve.wait_ge(hi_made, count)
                dve.tensor_tensor(w_lo[:, slot(u)].rearrange("p k c -> p (k c)"),
                                  raw[:, raw_slot(u)].rearrange("p k c -> p (k c)"),
                                  w_hi[:, slot(u)].rearrange("p k c -> p (k c)").bitcast(F32),
                                  ALU.subtract).then_inc(lo_made, 1)

            dve.memset(rows[:], 0.0).then_inc(rows_zero, 1)
            dve.memset(cols[:, 0:1], EPS).then_inc(cols_made, 1)
            dve.memset(cols[:, 1:2], 1.0).then_inc(cols_made, 1)
            dve.memset(qscale, float(SCALE2) ** 0.5).then_inc(cols_made, 1)
            dve.wait_ge(start_act, 4)
            dve.tensor_scalar(rst, ssq, 1.0 / D, EPS, ALU.mult, ALU.add).then_inc(start_dve, 1)
            dve.wait_ge(start_dve, 1)
            dve.reciprocal(rst, rst).then_inc(start_dve, 1)
            for i in range(3):
                dve.wait_ge(vecs_turned, 3)
                dve.tensor_copy(vecs[:, i * P:(i + 1) * P], ps[:, 0, i * P:(i + 1) * P]).then_inc(vecs_made, 1)
            dve.wait_ge(vecs_made, 3)
            l0, l1 = vecs[:, V_LB:V_LB + 8], vecs[:, V_LB + 8:V_LB + 16]
            dve.tensor_tensor(lbt[:, 0], l0, l1, ALU.max).then_inc(start_dve, 1)
            dve.wait_ge(start_dve, 3)
            dve.tensor_tensor(lbt[:, 1], l0, lbt[:, 0], ALU.subtract).then_inc(start_dve, 1)
            dve.tensor_tensor(lbt[:, 2], l1, lbt[:, 0], ALU.subtract).then_inc(start_dve, 1)
            dve.wait_ge(start_act, 10)
            dve.tensor_tensor(c_act, c_act, vecs[:, V_C:V_C + 8], ALU.mult).then_inc(start_dve, 1)
            dve.wait_ge(start_act, 11)
            dve.tensor_tensor(lbt[:, 3], lbt[:, 1], lbt[:, 2], ALU.add).then_inc(start_dve, 1)
            dve.wait_ge(start_dve, 7)
            dve.reciprocal(lbt[:, 4], lbt[:, 3]).then_inc(start_dve, 1)
            dve.wait_ge(start_dve, 8)
            dve.tensor_tensor(lb, lbt[:, 1], lbt[:, 4], ALU.mult).then_inc(start_dve, 1)
            dve.wait_ge(start_dve, 9)
            dve.tensor_scalar(omlb, lb, -1.0, 1.0, ALU.mult, ALU.add).then_inc(start_dve, 1)
            dve.wait_ge(cols_made, 3)
            dve.tensor_scalar(gnw, vecs[:, V_GNW:V_GNW + 2], qscale, None, ALU.mult).then_inc(start_dve, 1)
            dve.tensor_scalar(hnw, vecs[:, V_HNW:V_HNW + 1], qscale, None, ALU.mult).then_inc(start_dve, 1)
            for k in range(KT):
                dve.wait_ge(x_turned, 2 * k + 1)
                dve.tensor_copy(xT[:, k], ps[:, 2 * (k % 2) + 2]).then_inc(xT_made, 1)
            dve.wait_ge(ada0_used, 8)
            dve.tensor_tensor(ada[:, 0:16], ps[:, 6, 0:16], vecs[:, V_BADA:V_BADA + 16], ALU.add).then_inc(ada0_made, 1)
            dve.wait_ge(ada0_made, 1)
            dve.scalar_tensor_tensor(out=a_mix, in0=ada[:, 8:16], scalar=1.0, in1=vecs[:, V_NMIX:V_NMIX + 8],
                                     op0=ALU.add, op1=ALU.mult).then_inc(ada0_made, 1)
            dve.wait_ge(ada0_made, 2)
            split_lo(0, 1)
            for k in range(KT):
                dve.wait_ge(xnT_made, k + 1)
                dve.tensor_scalar(h_tmp[:, k % 2], xnT[:, k], a_mix[:, k:k + 1], ada[:, k:k + 1],
                                  ALU.mult, ALU.add).then_inc(h_tmp_made, 1)
                dve.wait_ge(h_tmp_made, k + 1)
                dve.wait_ge(h_hi_made, k + 1)
                dve.tensor_tensor(h_lo[:, k], h_tmp[:, k % 2], h_hi[:, k].bitcast(F32), ALU.subtract
                                  ).then_inc(h_lo_made, 1)
            for n in range(AHEAD):
                split_lo(U_MIX + n, U_MIX + n + 1)
            dve.wait_ge(xT_out, 16)
            dve.wait_ge(mask_made, 6)
            dve.wait_ge(gk2_in, 16)

            def decays(g, h, b):
                b3 = bcum[:, b].rearrange("p (c t) -> p c t", t=CHUNK)
                if h:
                    dve.wait_ge(ln_made, g * 2 + h)
                dve.wait_ge(exp_made, g * 15 + (0, 0, 5)[h])
                src = lg[:, max(h - 1, 0)]
                dve.tensor_tensor_scan(bcum[:, b], scan_mask[:], src, 0.0, ALU.mult, ALU.add).then_inc(scan_made, 1)
                dve.wait_ge(scan_made, g * 3 + h + 1)
                for dst, at in ((d_last, CHUNK - 1), (d_ref, CHUNK // 2 - 1)):
                    dve.tensor_tensor(dst[:, b].rearrange("p (c t) -> p c t", t=CHUNK), b3,
                                      b3[:, :, at:at + 1].to_broadcast([P, NCH, CHUNK]),
                                      ALU.subtract).then_inc(d_made, 1)

            def times_k(g, h):
                s = h % 2
                for i, e in enumerate((kp, ks)):
                    dve.wait_ge(exp_made, g * 15 + 5 * h + (1, 3)[i])
                    if h == 0:
                        ins = dve.tensor_tensor(e[:, s], e[:, s], key[:, 1], ALU.mult)
                    else:
                        ins = dve.scalar_tensor_tensor(out=e[:, s], in0=key[:, h - 1],
                                                       scalar=omlb[:, bass.ds(g * 2 + (h - 1), 1)], in1=e[:, s],
                                                       op0=ALU.mult, op1=ALU.mult)
                    ins.then_inc(kk_made, 1)

            def mask_scores(g, h):
                dve.wait_ge(scored, g * 3 + h + 1)
                dve.wait_ge(o_done, g * 4 + (0, 2, 3)[h])
                dve.memset(cols[:, 63:64], 0.0)
                dve.copy_predicated(sT[:], causal[:].bitcast(U32).unsqueeze(1).to_broadcast([P, TT, P]),
                                    ps[:, MISC_S[h]].rearrange("p (t i) -> p t i", i=P)).then_inc(sT_made, 1)

            def states(g, w, h):
                dve.wait_ge(o_done, g * 4 + w)
                for i in range(NCH - 1):
                    if i == 0:
                        dve.wait_ge(u_done, g * 4 + w + 1)
                    u = ps[:, B_STATE + i % 2, (i // 2) * P:(i // 2 + 1) * P]
                    if i == 0:
                        ins = dve.tensor_copy(state[:, 0], u)
                    else:
                        dve.wait_ge(state_made, g * 28 + 7 * w + i)
                        ins = dve.scalar_tensor_tensor(out=state[:, i], in0=state[:, i - 1],
                                                       scalar=decay[:, h, i:i + 1], in1=u,
                                                       op0=ALU.mult, op1=ALU.add)
                    ins.then_inc(state_made, 1)

            def silu(g, n, buf):
                dve.wait_ge(sig_made, g * 8 + (3, 4, 5, 6, 7, 8)[BY_DVE.index(n)])
                dve.tensor_tensor(buf, ps[:, B_PROJ + (U_MIX + n) % 2], buf, ALU.mult).then_inc(taken_dve, 1)

            def norm(g, w, i):
                dve.wait_ge(rn_made, g * 3 + i + 1)
                dve.wait_ge(o_taken, g * 4 + w + 1)
                dve.tensor_tensor(oe[:, w % 2], oe[:, w % 2], rn[:], ALU.mult).then_inc(normed, 1)

            with dve.Fori(0, GROUPS) as g:
                dve.wait_ge(z_done, g)
                dve.tensor_copy(gk2[0:LOWRANK, 0:P], gk2[32:32 + LOWRANK, bass.ds(g * P, P)]).then_inc(gk2_made, 1)
                for n in range(NU):
                    ms = [n + AHEAD] if (n in (0, 1) or n >= 5) else ([6, 7, 8] if n == 4 else [])
                    for m in ms:
                        split_lo(U_MIX + m, g * NU + U_MIX + m + 1)
                    if n == 3:
                        dve.wait_ge(z_done, g + 1)
                        dve.tensor_scalar(lg[:, 0], ps[:, MISC_Z], vecs[:, bass.ds(g + V_BGK, 1)], None, ALU.add
                                          ).then_inc(z_made, 1)
                        dve.wait_ge(soft_step, g * 3 + 3)
                        dve.scalar_tensor_tensor(out=lg[:, 0], in0=lg[:, 0], scalar=0.0, in1=lg[:, 1],
                                                 op0=ALU.min, op1=ALU.subtract).then_inc(la_made, 1)
                        dve.wait_ge(la_made, g + 1)
                        decays(g, 0, 0)
                    if n == 5:
                        dve.wait_ge(taken_act, g * N_ACT + taken_counts(5)[1] + 1)
                        times_k(g, 0)
                    if n == 6:
                        mask_scores(g, 0)
                    if n == 8:
                        silu(g, 8, qry[:, 0])
                        dve.wait_ge(ada_used, g * 8 + 8)
                        dve.tensor_tensor(ada[:, bass.ds(g * 8 + 16, 8)], ps[:, B_STATE + 1, 3 * P:3 * P + 8],
                                          vecs[:, bass.ds(g * 8 + V_BADA + 16, 8)], ALU.add).then_inc(ada_made, 1)
                        states(g, 0, 0)
                    if n == 9:
                        silu(g, 9, qry[:, 1])
                        decays(g, 1, 1)
                        states(g, 1, 0)
                        decays(g, 2, 0)
                    if n == 10:
                        times_k(g, 1)
                        silu(g, 10, gate[:, 0])
                    if n == 11:
                        times_k(g, 2)
                        mask_scores(g, 1)
                    if n == 12:
                        silu(g, 12, gate[:, 1])
                        states(g, 2, 1)
                    if n == 13:
                        norm(g, 0, 0)
                        norm(g, 1, 0)
                    if n == 14:
                        mask_scores(g, 2)
                        silu(g, 14, gate[:, 2])
                        states(g, 3, 2)
                    if n == 16:
                        silu(g, 16, gate[:, 3])
                        norm(g, 2, 1)
                    if n == 17:
                        norm(g, 3, 2)

            for k in range(KT):
                dve.wait_ge(m_hi_made, k + 1)
                dve.tensor_tensor(h_lo[:, k], merged[:, k], h_hi[:, k].bitcast(F32), ALU.subtract).then_inc(m_lo_made, 1)
            dve.wait_ge(xT_back, 16)
            for j in range(KT):
                u = U_OUT + j + AHEAD
                split_lo(u, u + 1)
                dve.wait_ge(proj_done, U_OUT + j + 1)
                dve.scalar_tensor_tensor(out=hres[:, j], in0=ps[:, B_PROJ + (U_OUT + j) % 2],
                                         scalar=ada[:, 16 + j:17 + j], in1=hres[:, j],
                                         op0=ALU.mult, op1=ALU.add).then_inc(hres_made, 1)
            dve.wait_ge(ada_made, GROUPS)
            dve.scalar_tensor_tensor(out=a_ffn, in0=ada[:, 32:40], scalar=1.0, in1=vecs[:, V_NFFN:V_NFFN + 8],
                                     op0=ALU.add, op1=ALU.mult).then_inc(a_ffn_made, 1)
            dve.wait_ge(const_made, 3)
            for j in range(KT):
                dve.tensor_scalar(prod[:, j // 4, (j % 4) * P:(j % 4 + 1) * P], ident[:], ada[:, 40 + j:41 + j], None,
                                  ALU.mult).then_inc(diag_made, 1)
            dve.wait_ge(a_ffn_made, 1)
            dve.wait_ge(rn2_step, 2)
            for k in range(KT):
                if k >= 2:
                    dve.wait_ge(n_hi_made, k - 1)
                dve.tensor_tensor(n_tmp[:, k % 2], hres[:, k], rn2[:], ALU.mult).then_inc(n_made, 1)
                dve.wait_ge(n_made, k + 1)
                dve.tensor_scalar(conv[:, k % 2], n_tmp[:, k % 2], a_ffn[:, k:k + 1], ada[:, 24 + k:25 + k],
                                  ALU.mult, ALU.add).then_inc(n_lo_made, 1)
                dve.wait_ge(n_lo_made, 2 * k + 1)
                dve.wait_ge(n_hi_made, k + 1)
                dve.tensor_tensor(h_lo[:, k], conv[:, k % 2], h_hi[:, k].bitcast(F32), ALU.subtract).then_inc(n_lo_made, 1)

            def taps(r, m, b, end):
                ch = r * 3 + (m // 2) + (m % 2) * FT if end is None else end + (m % 2) * FT
                dve.wait_ge(conv_a, r * 6 + b + 1)
                dve.scalar_tensor_tensor(out=conv[:, m, 1:T], in0=ps[:, m, 0:T - 1],
                                         scalar=vecs[:, bass.ds(ch + V_TAP1, 1)], in1=conv[:, m, 1:T],
                                         op0=ALU.mult, op1=ALU.add).then_inc(conv_b_, 1)
                dve.wait_ge(conv_b_, r * 6 + b + 1)
                dve.scalar_tensor_tensor(out=conv[:, m, 2:T], in0=ps[:, m, 0:T - 2],
                                         scalar=vecs[:, bass.ds(ch + V_TAP0, 1)], in1=conv[:, m, 2:T],
                                         op0=ALU.mult, op1=ALU.add).then_inc(conv_made, 1)

            with dve.Fori(0, 7) as r:
                for m in range(6):
                    u = U_UP + m + AHEAD
                    split_lo(u, r * 6 + u + 1)
                    taps(r, m, m, None)
            for m in range(2):
                u = U_UP + 42 + m + AHEAD
                split_lo(u, u + 1)
                taps(0, m, 42 + m, 21)

            def prod_lo(r, f):
                dve.wait_ge(p_hi_made, r * 6 + f + 1)
                dve.tensor_tensor(h_lo[:, f % 6], prod[:, bass.ds(r * 6 + f, 1), :].rearrange("p a t -> p (a t)"),
                                  h_hi[:, f % 6].bitcast(F32), ALU.subtract).then_inc(p_lo_made, 1)

            for f in range(AHEAD):
                prod_lo(0, f)
            with dve.Fori(0, 3) as r:
                for m in range(6):
                    u = U_DOWN + m + AHEAD
                    split_lo(u, r * 6 + u + 1)
                    prod_lo(r, m + AHEAD)
            dve.wait_ge(gf_made, 1)
            dve.wait_ge(fw_in, 16)
            dve.wait_ge(ht_made, TT)
            for t in range(TT):
                dve.wait_ge(y_done, t + 1)
                y = prod[:, 2 + 2 * (t % 2):4 + 2 * (t % 2)]
                dve.tensor_tensor(y, ps[:, 2 * t:2 * t + 2], gf_b[:].rearrange("p (a b) -> p a b", a=2), ALU.mult
                                  ).then_inc(fin_step, 1)
                dve.wait_ge(fin_step, 2 * t + 1)
                dve.tensor_tensor(hres_tok[:, t], hres_tok[:, t], y.rearrange("p a t -> p (a t)"), ALU.add
                                  ).then_inc(fin_step, 1)
                dve.wait_ge(fsq_made, 2 * t + 1)
                dve.tensor_scalar(frs[:, t:t + 1], fss[:, t:t + 1], 1.0 / D, EPS, ALU.mult, ALU.add).then_inc(frs_made, 1)
                dve.wait_ge(frs_made, 2 * t + 1)
                dve.reciprocal(frs[:, t:t + 1], frs[:, t:t + 1]).then_inc(frs_made, 1)
                dve.wait_ge(fsq_made, 2 * t + 2)
                dve.scalar_tensor_tensor(out=hres_tok[:, t], in0=hres_tok[:, t], scalar=frs[:, t:t + 1], in1=fw_b[:],
                                         op0=ALU.mult, op1=ALU.mult).then_inc(fin_made, 1)

        @block.tensor
        def _(pe):
            def three(dst, pairs, start=True, stop=True):
                n = len(pairs)
                for i, ((a_hi, a_lo), (b_hi, b_lo)) in enumerate(pairs):
                    pe.matmul(dst, a_hi, b_hi, start=start and i == 0, stop=False)
                    pe.matmul(dst, a_hi, b_lo, start=False, stop=False)
                    last = pe.matmul(dst, a_lo, b_hi, start=False, stop=stop and i == n - 1)
                return last

            def unit(u, bank):
                s = slot(u)
                return three(ps[:, bank], [((w_hi[:, s, k], w_lo[:, s, k]), (h_hi[:, k], h_lo[:, k]))
                                           for k in range(KT)])

            pe.wait_ge(rows_in, 16 * 11)
            pe.wait_ge(const_made, 3)
            for i in range(3):
                pe.transpose(ps[:, 0, i * P:(i + 1) * P], rows[:, i], ident[:]).then_inc(vecs_turned, 1)
            pe.wait_ge(x_in, 16)
            pe.wait_ge(start_act, 9)
            for k in range(KT):
                if k >= 2:
                    pe.wait_ge(xT_made, k - 1)
                    pe.wait_ge(xnT_made, k - 1)
                for i, src in enumerate((x_tok, xn_tok)):
                    for t in range(TT):
                        last = pe.transpose(ps[:, 2 + 2 * (k % 2) + i, t * P:(t + 1) * P],
                                            src[:, t, k * P:(k + 1) * P], ident[:])
                    last.then_inc(x_turned, 1)
            pe.wait_ge(start_dve, 6)
            for i in range(8):
                pe.wait_ge(ada0_in[i % 4], 16 * (i // 4 + 1))
                for m in range(2):
                    for k in range(KT):
                        last = pe.matmul(ps[:, 6, 2 * i + m:2 * i + m + 1], ada_w0[:, i % 4, k, m * P:(m + 1) * P],
                                         c_act[:, k:k + 1], start=k == 0, stop=k == KT - 1)
                last.then_inc(ada0_used, 1)
            pe.wait_ge(vecs_made, 3)
            pe.wait_ge(lo_made, 1)
            for k in range(KT):
                pe.wait_ge(h_lo_made, k + 1)
                last = three(ps[:, B_PROJ], [((w_hi[:, slot(0), k], w_lo[:, slot(0), k]), (h_hi[:, k], h_lo[:, k]))],
                             start=k == 0, stop=k == KT - 1)
            last.then_inc(proj_done, 1)

            def turn(g, h):
                pe.wait_ge(kk_made, g * 6 + 2 * h + 1)
                for t in range(TT):
                    last = pe.transpose(ps[:, MISC_T[h], t * P:(t + 1) * P], kp[:, h % 2, t * P:(t + 1) * P], ident[:])
                last.then_inc(turned, 1)

            def score(g, h):
                pe.wait_ge(kk_made, g * 6 + 2 * h + 2)
                pe.wait_ge(qq_made, g * 6 + 2 * h + 1)
                half = CHUNK // 2
                for t in range(TT):
                    for j in range(0, P, half):
                        i = slice(t * P + j, t * P + (j // CHUNK + 1) * CHUNK)
                        last = pe.matmul(ps[j:j + half, MISC_S[h], i], ks[:, h % 2, t * P + j:t * P + j + half],
                                         qs[:, h % 2, i], start=True, stop=True)
                last.then_inc(scored, 1)

            def chunk_states(g, w, h):
                pe.wait_ge(kT_made, g * 3 + h + 1)
                pe.wait_ge(state_made, g * 28 + 7 * w)
                for i in range(NCH - 1):
                    if w == 0 and i == 1:
                        pe.wait_ge(ada_made, g + 1)
                    rows_ = slice(CHUNK * (i % 2), CHUNK * (i % 2) + CHUNK)
                    last = pe.matmul(ps[:, B_STATE + i % 2, (i // 2) * P:(i // 2 + 1) * P], kT[rows_, i // 2],
                                     v[rows_, i // 2, w * P:(w + 1) * P], start=True, stop=True)
                last.then_inc(u_done, 1)

            def outputs(g, w, h):
                pe.wait_ge(sT_made, g * 3 + h + 1)
                pe.wait_ge(qq_made, g * 6 + 2 * h + 2)
                pe.wait_ge(o_taken, g * 4 + max(w - 1, 0))
                for t in range(TT):
                    o = ps[:, B_O + w % 2, t * P:(t + 1) * P]
                    pe.matmul(o, v[:, t, w * P:(w + 1) * P], sT[:, t], start=True, stop=False)
                    for i in (2 * t, 2 * t + 1):
                        if i:
                            pe.wait_ge(state_made, g * 28 + 7 * w + i)
                            last = pe.matmul(o[:, (i % 2) * CHUNK:(i % 2 + 1) * CHUNK], state[:, i - 1],
                                             qe[:, h % 2, i * CHUNK:(i + 1) * CHUNK], start=False, stop=i % 2 == 1)
                last.then_inc(o_done, 1)

            def square_sums(g, i, tiles):
                for j, w in enumerate(tiles):
                    pe.wait_ge(sq_made, g * 4 + w + 1)
                    last = pe.matmul(ps[:, MISC_SS[i]], ones[:], sq[:, w % 2], start=j == 0, stop=j == len(tiles) - 1)
                last.then_inc(ss_done, 1)

            def group(g, first):
                for n in range(NU):
                    u = U_MIX + n
                    if n == 0:
                        pe.wait_ge(lo_made, g * NU + U_MIX + 4)
                    elif n >= 4:
                        pe.wait_ge(lo_made, g * NU + u + 1)
                    if not (first and n == 0):
                        if first and n == 1:
                            pe.wait_ge(taken_act, 1)
                        else:
                            prod_wait(pe, g, n)
                    bank = B_PROJ + u % 2
                    if n < 4:
                        tok = slice(n * P, (n + 1) * P)
                        last = three(ps[:, bank].rearrange("p (a b) -> p a b", b=P), [((h_hi[:, k, tok], h_lo[:, k, tok]),
                                                    (w_hi[:, 0:4, k], w_lo[:, 0:4, k])) for k in range(KT)])
                    else:
                        last = unit(u, bank)
                    last.then_inc(proj_done, 1)
                    if 1 <= n < 9:
                        m = n - 1
                        if m == 0:
                            pe.wait_ge(state_made, g * 28)
                            pe.wait_ge(ada_made, g)
                        pe.wait_ge(ada_in[m % 2], (g * 4 + m // 2 + 1) * 16)
                        for k in range(KT):
                            last = pe.matmul(ps[:, B_STATE + 1, 3 * P + m:3 * P + m + 1], ada_w[:, m % 2, k],
                                             c_act[:, k:k + 1], start=k == 0, stop=k == KT - 1)
                        last.then_inc(ada_used, 1)
                    if n == 2:
                        pe.wait_ge(gk2_made, g + 1)
                        pe.wait_ge(taken_act, g * N_ACT + 1)
                        pe.wait_ge(ss_taken, g * 3)
                        pe.matmul(ps[:, MISC_Z], gk2[0:LOWRANK, 0:P], lrT[:], start=True, stop=True).then_inc(z_done, 1)
                    if n == 6:
                        score(g, 0)
                    if n == 7:
                        pe.wait_ge(z_made, g + 1)
                        turn(g, 0)
                    if n == 8:
                        chunk_states(g, 0, 0)
                    if n == 9:
                        outputs(g, 0, 0)
                        chunk_states(g, 1, 0)
                    if n == 10:
                        outputs(g, 1, 0)
                    if n == 11:
                        pe.wait_ge(sT_made, g * 3 + 1)
                        turn(g, 1)
                        pe.wait_ge(kT_made, g * 3 + 1)
                        score(g, 1)
                    if n == 12:
                        chunk_states(g, 2, 1)
                        square_sums(g, 0, (0, 1))
                    if n == 13:
                        outputs(g, 2, 1)
                        pe.wait_ge(sT_made, g * 3 + 2)
                        turn(g, 2)
                    if n == 14:
                        pe.wait_ge(ss_taken, g * 3 + 1)
                        score(g, 2)
                        chunk_states(g, 3, 2)
                    if n == 15:
                        outputs(g, 3, 2)
                        pe.wait_ge(kT_made, g * 3 + 3)
                        square_sums(g, 1, (2,))
                    if n == 17:
                        pe.wait_ge(sT_made, g * 3 + 3)
                        square_sums(g, 2, (3,))

            group(0, True)
            with pe.Fori(1, GROUPS) as g:
                group(g, False)

            def residual_square(j):
                pe.wait_ge(sq2_made, j + 1)
                if j == 0:
                    pe.wait_ge(ss_taken, 3 * GROUPS)
                pe.matmul(ps[:, B_MISC], ones[:], n_tmp[:, j % 2], start=j == 0, stop=j == KT - 1).then_inc(ss2_step, 1)

            for j in range(KT):
                u = U_OUT + j
                pe.wait_ge(lo_made, u + 1)
                if j == 0:
                    pe.wait_ge(taken_dve, GROUPS * N_DVE)
                if j < 2:
                    pe.wait_ge(taken_act, GROUPS * N_ACT + 1)
                else:
                    pe.wait_ge(hres_made, j - 1)
                for k in range(KT):
                    if j == 0:
                        pe.wait_ge(m_lo_made, k + 1)
                    last = three(ps[:, B_PROJ + u % 2],
                                 [((w_hi[:, slot(u), k], w_lo[:, slot(u), k]), (h_hi[:, k], h_lo[:, k]))],
                                 start=k == 0, stop=k == KT - 1)
                last.then_inc(proj_done, 1)
                if j:
                    residual_square(j - 1)
            residual_square(KT - 1)
            pe.wait_ge(diag_made, KT)
            pe.wait_ge(o_taken, 4 * GROUPS)
            for j in range(KT):
                last = pe.matmul(ps[:, B_O + j // 4, (j % 4) * P:(j % 4 + 1) * P], ones[:],
                                 prod[:, j // 4, (j % 4) * P:(j % 4 + 1) * P], start=True, stop=True)
            last.then_inc(gf_done, 1)

            def up_unit(r, m, b):
                u = U_UP + m
                pe.wait_ge(lo_made, r * 6 + U_UP + b + 1)
                return unit(u, m)

            for m in range(6):
                u = U_UP + m
                pe.wait_ge(lo_made, u + 1)
                for k in range(KT):
                    if m == 0:
                        pe.wait_ge(n_lo_made, 2 * k + 2)
                    last = three(ps[:, m], [((w_hi[:, slot(u), k], w_lo[:, slot(u), k]), (h_hi[:, k], h_lo[:, k]))],
                                 start=k == 0, stop=k == KT - 1)
                last.then_inc(proj_done, 1)
                if m < TT:
                    t = m
                    if t == 0:
                        pe.wait_ge(gf_made, 1)
                    else:
                        pe.wait_ge(ht_made, t)
                    for k in range(KT):
                        last = pe.transpose(ps[:, B_O + k // 4, (k % 4) * P:(k % 4 + 1) * P],
                                            hres[:, k, t * P:(t + 1) * P], ident[:])
                    last.then_inc(ht_done, 1)
            with pe.Fori(1, 7) as r:
                for m in range(6):
                    pe.wait_ge(conv_made, r * 6 + m - 5)
                    up_unit(r, m, m).then_inc(proj_done, 1)
            for m in range(2):
                pe.wait_ge(conv_made, 42 + m - 5)
                up_unit(0, m, 42 + m).then_inc(proj_done, 1)

            def down(f_slot, u, t, half, start=False, stop=False):
                s = slot(u)
                tok = slice(t * P, (t + 1) * P)
                cols_ = slice(4 * half, 4 * half + 4)
                return three(ps[:, 2 * t + half].rearrange("p (a b) -> p a b", b=P),
                             [((h_hi[:, f_slot, tok], h_lo[:, f_slot, tok]),
                               (w_hi[:, s, cols_], w_lo[:, s, cols_]))], start=start, stop=stop)

            def down_unit(f, start):
                for t in range(TT):
                    for half in range(2):
                        last = down(f % 6, U_DOWN + f, t, half, start=start)
                last.then_inc(proj_done, 1)

            pe.wait_ge(conv_made, 2 * FT)
            pe.wait_ge(ht_made, TT)
            pe.wait_ge(lo_made, U_DOWN + 1)
            pe.wait_ge(p_lo_made, 1)
            down_unit(0, True)
            with pe.Fori(0, 3) as r:
                for m in range(1, 7):
                    pe.wait_ge(lo_made, r * 6 + U_DOWN + m + 1)
                    pe.wait_ge(p_lo_made, r * 6 + m + 1)
                    down_unit(m, False)
            pe.wait_ge(lo_made, U_END)
            pe.wait_ge(p_lo_made, FT)
            for t in range(TT):
                for f in range(19, FT):
                    for half in range(2):
                        last = down(f % 6, U_DOWN + f, t, half, stop=f == FT - 1)
                last.then_inc(y_done, 1)


_INS = ["x", "c", "w_ada", "b_ada", "norm_mix_w", "w_in", "w_gk2", "b_gk2", "gla_norm_w", "hgrn_lb",
        "hgrn_norm_w", "w_out", "norm_ffn_w", "w_up", "conv_w", "conv_b", "w_down", "final_norm_w"]


def kernel(**inputs):
    import numpy as np
    import concourse.bacc as bacc
    from concourse.bass_utils import run_bass_kernel_spmd as run

    nc = bacc.Bacc("TRN2", target_bir_lowering=False, num_devices=1)
    arrays, args = {}, []
    for name in _INS:
        a = np.ascontiguousarray(inputs[name])
        arrays[f"in_{name}_dram"] = a
        args.append(nc.dram_tensor(f"in_{name}_dram", a.shape, mybir.dt.from_np(a.dtype), kind="ExternalInput").ap())
    out = nc.dram_tensor("out_dram", (1, T, D), F32, kind="ExternalOutput").ap()
    build(nc, *args, out)
    r = run(nc, [arrays], core_ids=[0])
    return r.results[0]["out_dram"]
```

```python
from contextlib import ExitStack

import concourse.bass as bass
from concourse import mybir

F32 = mybir.dt.float32
F32R = mybir.dt.float32r
BF16 = mybir.dt.bfloat16
U32 = mybir.dt.uint32
ALU = mybir.AluOpType
ACT = mybir.ActivationFunctionType

P = 128
D = 1024
T = 512
KT = D // P
TT = T // P
CHUNK = 64
NCH = T // CHUNK
GROUPS = 4
D_FF = 2816
FT = D_FF // P
GLA_QK, GLA_V, LOWRANK = 512, 1024, 16
GLA_DV = GLA_V // GROUPS
HGRN_DV = 128
LOGIT_NORM = 16.0
SCALE2 = 1.0 / 128
EPS = 1e-6

GQ, GK, GV, GG = 0, GLA_QK, 2 * GLA_QK, 2 * GLA_QK + GLA_V
GLR = GG + GLA_V
HQ = GLR + LOWRANK
HF, HI, HG, MA, MB = (HQ + i * D for i in range(1, 6))
UNITS = [(GV, 256), (GV + P, 256), (HI, 256), (HI + P, 256), (GQ, P), (GK, P),
         (HF, 256), (HF + P, 256), (HQ, 256), (HQ + P, 256),
         (GG, 256), (MA, 256), (GG + P, 256), (MA + P, 256),
         (HG, 256), (MB, 256), (HG + P, 256), (MB + P, 256)]
NU = len(UNITS)
U_MIX = 1
U_OUT = U_MIX + GROUPS * NU
U_UP = U_OUT + KT
U_DOWN = U_UP + 2 * FT
U_END = U_DOWN + FT
RING, RAW = 6, 3
AHEAD = 4
BY_DVE = (8, 9, 10, 12, 14, 16)

B_PROJ, B_MISC, B_STATE, B_O = 0, 2, 4, 6
OUT_BANKS = (0, 1, 4, 5)
MISC_Z = 2
MISC_T = (2, 3, 2)
MISC_S = (3, 2, 3)
MISC_SS = (3, 2, 3)

V_BADA, V_NMIX, V_NFFN, V_CONVB, V_LB, V_BGK = 0, 48, 56, 64, 108, 124
V_TAP0, V_TAP1, V_C, V_GNW, V_HNW, V_TAP2 = 128, 172, 216, 224, 226, 256


def slot(u):
    return (u + 5) % RING


def raw_slot(u):
    return (u + 2) % RAW


def raw_count(u):
    return u // RAW + 1


def taken_counts(n):
    if n in BY_DVE:
        return True, BY_DVE.index(n) + 1
    return False, len([m for m in range(n + 1) if m not in BY_DVE])


N_DVE = len(BY_DVE)
N_ACT = NU - N_DVE


def build(nc, x, c, w_ada, b_ada, norm_mix_w, w_in, w_gk2, b_gk2, gla_norm_w, hgrn_lb, hgrn_norm_w,
          w_out, norm_ffn_w, w_up, conv_w, conv_b, w_down, final_norm_w, out):
    ctx = ExitStack()
    with ctx:
        def sem(name):
            return ctx.enter_context(nc.semaphore(name))

        def sbuf(stack):
            def alloc(name, shape, dt=F32):
                return stack.enter_context(nc.sbuf_tensor(name, shape, dt))
            return alloc

        sb = sbuf(ctx)
        raw = sb("raw", [P, RAW, KT, P])
        w_hi = sb("w_hi", [P, RING, KT, P], F32R)
        w_lo = sb("w_lo", [P, RING, KT, P], F32R)
        h_hi = sb("h_hi", [P, KT, T], F32R)
        h_lo = sb("h_lo", [P, KT, T], F32R)
        vecs = sb("vecs", [P, 3 * P])
        ada = sb("ada", [P, 48])
        ident = sb("ident", [P, P])
        ones = sb("ones", [P, P])
        cols = sb("cols", [P, 64])
        eps_c, one_c = cols[:, 0:1], cols[:, 1:2]
        c_act = cols[:, 2:10]
        a_mix = cols[:, 10:18]
        lb, omlb = cols[:, 18:26], cols[:, 26:34]
        a_ffn = cols[:, 34:42]
        gnw, hnw = cols[:, 42:44], cols[:, 44:45]
        ssq, rst = cols[:, 45:49], cols[:, 49:53]
        qscale = cols[:, 53:54]
        frs = cols[:, 54:58]
        fss = sb("fss", [P, 2 * TT])

        init = ExitStack()
        si = sbuf(init)
        rows = si("rows", [P, 3, P])
        x_tok = si("x_tok", [P, TT, D])
        xn_tok = si("xn_tok", [P, TT, D])
        xnT = si("xnT", [P, KT, T])
        xT = si("xT", [P, KT, T])
        ada_w0 = si("ada_w0", [P, 4, 2 * D])
        ada_acc0 = si("ada_acc0", [P, 2 * D])
        h_tmp = si("h_tmp", [P, 2, T])
        lbt = si("lbt", [P, 5, KT])
        init.close()

        mix = ExitStack()
        sm = sbuf(mix)
        merged = sm("merged", [P, KT, T])
        ada_w = sm("ada_w", [P, 2, D])
        ada_acc = sm("ada_acc", [P, D])
        v = sm("v", [P, TT, 4 * P])
        qs = sm("qs", [P, 2, T])
        ks = sm("ks", [P, 2, T])
        qe = sm("qe", [P, 2, T])
        kp = sm("kp", [P, 2, T])
        bcum = sm("bcum", [P, 2, T])
        d_ref = sm("d_ref", [P, 2, T])
        d_last = sm("d_last", [P, 2, T])
        lg = sm("lg", [P, 2, T])
        key = sm("key", [P, 2, T])
        qry = sm("qry", [P, 2, T])
        decay = sm("decay", [P, 3, NCH])
        kT = sm("kT", [P, TT, P])
        sT = sm("sT", [P, TT, P])
        state = sm("state", [P, NCH - 1, P])
        gate = sm("gate", [P, 4, T])
        gmul = sm("gmul", [P, T])
        sq = sm("sq", [P, 2, T])
        oe = sm("oe", [P, 2, T])
        rn = sm("rn", [P, T])
        lrT = sm("lrT", [LOWRANK, T])
        gk2 = sm("gk2", [32 + LOWRANK, T])
        scan_mask = sm("scan_mask", [P, T], BF16)
        causal = sm("causal", [P, P])
        mix.close()

        sf = sbuf(ctx)
        prod = sf("prod", [P, FT, T])
        hres = sf("hres", [P, KT, T])
        hres_tok = sf("hres_tok", [P, TT, D])
        conv = sf("conv", [P, 6, T])
        n_tmp = sf("n_tmp", [P, 2, T])
        rn2 = sf("rn2", [P, T])
        fw_b = sf("fw_b", [P, D])
        gf_b = sf("gf_b", [P, D])
        xT_dram = nc.dram_tensor("xT_saved_dram", [P, KT, T], F32, kind="Internal").ap()

        ps = ctx.enter_context(nc.psum_tensor("ps", [P, 8, T], F32))

        rows_zero = sem("rows_zero")
        rows_in = sem("rows_in")
        x_in = sem("x_in")
        gk2_in = sem("gk2_in")
        fw_in = sem("fw_in")
        ada0_in = [sem(f"ada0_in{i}") for i in range(4)]
        ada_in = [sem(f"ada_in{i}") for i in range(2)]
        raw_in = [sem(f"raw_in{i}") for i in range(RAW)]
        xT_out = sem("xT_out")
        xT_back = sem("xT_back")
        out_done = sem("out_done")
        const_made = sem("const_made")
        cols_made = sem("cols_made")
        mask_made = sem("mask_made")
        vecs_turned = sem("vecs_turned")
        vecs_made = sem("vecs_made")
        start_act = sem("start_act")
        start_dve = sem("start_dve")
        x_turned = sem("x_turned")
        xT_made = sem("xT_made")
        xnT_made = sem("xnT_made")
        ada0_used = sem("ada0_used")
        ada0_summed = sem("ada0_summed")
        ada0_made = sem("ada0_made")
        ada_summed = sem("ada_summed")
        h_tmp_made = sem("h_tmp_made")
        h_hi_made = sem("h_hi_made")
        h_lo_made = sem("h_lo_made")
        hi_made = sem("hi_made")
        lo_made = sem("lo_made")
        proj_done = sem("proj_done")
        taken_act = sem("taken_act")
        taken_dve = sem("taken_dve")
        ada_used = sem("ada_used")
        ada_made = sem("ada_made")
        gk2_made = sem("gk2_made")
        z_done = sem("z_done")
        z_made = sem("z_made")
        soft_step = sem("soft_step")
        ln_made = sem("ln_made")
        sig_made = sem("sig_made")
        la_made = sem("la_made")
        scan_made = sem("scan_made")
        d_made = sem("d_made")
        exp_made = sem("exp_made")
        kk_made = sem("kk_made")
        qq_made = sem("qq_made")
        turned = sem("turned")
        kT_made = sem("kT_made")
        scored = sem("scored")
        sT_made = sem("sT_made")
        u_done = sem("u_done")
        state_made = sem("state_made")
        o_done = sem("o_done")
        o_taken = sem("o_taken")
        sq_made = sem("sq_made")
        sq_summed = sem("sq_summed")
        ss_done = sem("ss_done")
        ss_taken = sem("ss_taken")
        rn_made = sem("rn_made")
        normed = sem("normed")
        gated = sem("gated")
        y_made = sem("y_made")
        merged_made = sem("merged_made")
        m_hi_made = sem("m_hi_made")
        m_lo_made = sem("m_lo_made")
        hres_made = sem("hres_made")
        sq2_made = sem("sq2_made")
        sq2_summed = sem("sq2_summed")
        ss2_done = sem("ss2_done")
        ha_made = sem("ha_made")
        rn2_step = sem("rn2_step")
        a_ffn_made = sem("a_ffn_made")
        n_made = sem("n_made")
        n_hi_made = sem("n_hi_made")
        n_lo_made = sem("n_lo_made")
        diag_made = sem("diag_made")
        gf_done = sem("gf_done")
        gf_made = sem("gf_made")
        ht_done = sem("ht_done")
        ht_made = sem("ht_made")
        conv_a = sem("conv_a")
        conv_b_ = sem("conv_b_")
        conv_made = sem("conv_made")
        gate_made = sem("gate_made")
        prod_made = sem("prod_made")
        p_hi_made = sem("p_hi_made")
        p_lo_made = sem("p_lo_made")
        y_done = sem("y_done")
        fin_step = sem("fin_step")
        fsq_made = sem("fsq_made")
        frs_made = sem("frs_made")
        fin_made = sem("fin_made")

        def unit_view(w):
            return w[0].rearrange("(k p) c -> p k c", p=P)

        win_v, wout_v, wup_v, wada_v = map(unit_view, (w_in, w_out, w_up, w_ada))
        wdown_v = w_down[0].rearrange("(f p) n -> f p n", p=P)

        def prod_wait(eng, g, n):
            m = n - 2
            gg = g
            if m < 0:
                m, gg = m + NU, g - 1
            dve, k = taken_counts(m)
            if dve:
                eng.wait_ge(taken_dve, gg * N_DVE + k)
            else:
                eng.wait_ge(taken_act, gg * N_ACT + k + 1)

        block = ctx.enter_context(nc.Block())

        @block.sync
        def _(sp):
            sp.wait_ge(rows_zero, 1)
            def row(dst, src, n):
                sp.dma_start(rows[dst % P:dst % P + n, dst // P, :], src).then_inc(rows_in, 16)
            row(V_C, c[0].rearrange("(r p) -> r p", p=P), 8)
            row(V_BADA, b_ada[0].rearrange("(r p) -> r p", p=P), 48)
            row(V_NMIX, norm_mix_w[0].rearrange("(r p) -> r p", p=P), 8)
            row(V_NFFN, norm_ffn_w[0].rearrange("(r p) -> r p", p=P), 8)
            row(V_CONVB, conv_b[0].rearrange("(r p) -> r p", p=P), 44)
            row(V_LB, hgrn_lb.rearrange("a (r p) -> (a r) p", p=P), 16)
            row(V_BGK, b_gk2[0].rearrange("(r p) -> r p", p=P), 4)
            row(V_TAP0, conv_w[0, 0:2].rearrange("a (r p) -> (a r) p", p=P), 88)
            row(V_GNW, gla_norm_w[0].rearrange("(r p) -> r p", p=P), 2)
            row(V_HNW, hgrn_norm_w[0].rearrange("(r p) -> r p", p=P), 1)
            row(V_TAP2, conv_w[0, 2].rearrange("(r p) -> r p", p=P), 44)
            for k in range(KT):
                if k >= 4:
                    sp.wait_ge(ada0_used, k - 3)
                sp.dma_start(ada_w0[:, k % 4], wada_v[:, k, 0:2 * D]).then_inc(ada0_in[k % 4], 16)
                if k == 5:
                    sp.dma_start(raw[:, raw_slot(0)], win_v[:, :, GLR:GLR + P]).then_inc(raw_in[raw_slot(0)], 16)
                    for n in range(2):
                        c0 = UNITS[n][0]
                        sp.dma_start(raw[:, raw_slot(U_MIX + n)], win_v[:, :, c0:c0 + P]
                                     ).then_inc(raw_in[raw_slot(U_MIX + n)], 16)
            sp.wait_ge(xT_made, KT)
            sp.dma_start(xT_dram, xT[:]).then_inc(xT_out, 16)

            def load(u, src, free):
                sp.wait_ge(lo_made, free)
                sp.dma_start(raw[:, raw_slot(u)], src).then_inc(raw_in[raw_slot(u)], 16)

            def group_loads(g, first):
                for n in range(NU):
                    c0, step = UNITS[n]
                    u = U_MIX + n
                    if not (first and u < RAW):
                        load(u, win_v[:, :, bass.ds(g * step + c0, P)], g * NU + u - RAW + 1)
                    if 5 <= n < 13:
                        m = n - 5
                        if not (first and m < 2):
                            sp.wait_ge(ada_used, g * 8 + m - 1)
                        elif m == 0:
                            sp.wait_ge(xT_out, 16)
                            sp.wait_ge(proj_done, 1)
                        sp.dma_start(ada_w[:, m % 2], wada_v[:, m, bass.ds(g * D + 2 * D, D)]
                                     ).then_inc(ada_in[m % 2], 16)

            group_loads(0, True)
            with sp.Fori(1, GROUPS) as g:
                group_loads(g, False)
            for j in range(KT):
                load(U_OUT + j, wout_v[:, :, j * P:(j + 1) * P], U_OUT + j - RAW + 1)
                if j == 5:
                    sp.wait_ge(m_lo_made, KT)
                    sp.dma_start(hres[:], xT_dram).then_inc(xT_back, 16)
                    sp.dma_start(fw_b[:], final_norm_w.rearrange("(a d) -> a d", a=1).to_broadcast([P, D])
                                 ).then_inc(fw_in, 16)
            with sp.Fori(0, 7) as r:
                for m in range(6):
                    u = U_UP + m
                    load(u, wup_v[:, :, bass.ds(r * 3 * P + (m // 2) * P + (m % 2) * D_FF, P)],
                         r * 6 + u - RAW + 1)
            for m in range(2):
                u = U_UP + 42 + m
                load(u, wup_v[:, :, 21 * P + m * D_FF:22 * P + m * D_FF], u - RAW + 1)
            with sp.Fori(0, 3) as r:
                for m in range(6):
                    u = U_DOWN + m
                    load(u, wdown_v[bass.ds(r * 6 + m, 1)].rearrange("a p n -> (a p) n"), r * 6 + u - RAW + 1)
            for f in range(18, FT):
                u = U_DOWN + f
                load(u, wdown_v[f], u - RAW + 1)
            for t in range(TT):
                for half in range(2):
                    sp.wait_ge(fin_made, 2 * t + half + 1)
                    d = slice(half * T, (half + 1) * T)
                    sp.dma_start(out[0, t * P:(t + 1) * P, d], hres_tok[:, t, d]).then_inc(out_done, 16)
            sp.wait_ge(out_done, 16 * 2 * TT)

        @block.gpsimd
        def _(pool):
            pool.memset(ones[:], 1.0).then_inc(const_made, 1)
            pool.memset(ident[:], 0.0).then_inc(const_made, 1)
            pool.wait_ge(const_made, 2)
            pool.affine_select(out=ident[:], in_=ident[:], compare_op=ALU.not_equal, fill=1.0, base=0,
                               pattern=[[-1, P]], channel_multiplier=1).then_inc(const_made, 1)
            pool.wait_ge(xT_out, 16)
            pool.wait_ge(proj_done, 1)
            pool.dma_start(gk2[32:32 + LOWRANK, :], w_gk2[0]).then_inc(gk2_in, 16)
            pool.memset(scan_mask[:], 1.0).then_inc(mask_made, 1)
            pool.memset(causal[:], 1.0).then_inc(mask_made, 1)
            pool.wait_ge(mask_made, 2)
            pool.memset(scan_mask[:].rearrange("p (c t) -> p c t", t=CHUNK)[:, :, 0:1], 0.0).then_inc(mask_made, 1)
            pool.affine_select(out=causal[:], in_=causal[:], compare_op=ALU.is_ge, fill=0.0, base=0,
                               pattern=[[1, P]], channel_multiplier=-1).then_inc(mask_made, 1)
            pool.wait_ge(mask_made, 4)
            pool.memset(causal[0:CHUNK, CHUNK:P], 0.0).then_inc(mask_made, 1)
            pool.memset(sT[:], 0.0).then_inc(mask_made, 1)
            def times_q(g, h, q):
                s = h % 2
                pool.wait_ge(exp_made, g * 15 + 5 * h + 4)
                pool.tensor_tensor(qs[:, s], qs[:, s], q, ALU.mult).then_inc(qq_made, 1)
                pool.wait_ge(exp_made, g * 15 + 5 * h + 5)
                pool.tensor_tensor(qe[:, s], qe[:, s], q, ALU.mult).then_inc(qq_made, 1)

            def gate_mul(g, w):
                pool.wait_ge(taken_dve, g * N_DVE + taken_counts(10 + 2 * w)[1])
                pool.wait_ge(taken_act, g * N_ACT + taken_counts(11 + 2 * w)[1] + 1)
                pool.tensor_tensor(gate[:, w], gate[:, w], gmul[:], ALU.mult).then_inc(gated, 1)

            def gated_y(g, w):
                pool.wait_ge(gated, g * 4 + w + 1)
                pool.wait_ge(normed, g * 4 + w + 1)
                pool.tensor_tensor(gate[:, w], gate[:, w], oe[:, w % 2], ALU.mult).then_inc(y_made, 1)

            def merge(g, w):
                pool.wait_ge(y_made, g * 4 + w + 1)
                pool.tensor_tensor(merged[:, bass.ds(g * 2 + (w - 2), 1), :].rearrange("p a t -> p (a t)"),
                                   gate[:, w - 2], gate[:, w], ALU.add).then_inc(merged_made, 1)

            with pool.Fori(0, GROUPS) as g:
                pool.wait_ge(taken_act, g * N_ACT + taken_counts(5)[1] + 1)
                times_q(g, 0, qry[:, 1])
                pool.wait_ge(taken_dve, g * N_DVE + 1)
                times_q(g, 1, qry[:, 0])
                pool.wait_ge(taken_dve, g * N_DVE + 2)
                times_q(g, 2, qry[:, 1])
                pool.wait_ge(sq_made, g * 4 + 2)
                pool.tensor_tensor(sq[:, 0], sq[:, 0], sq[:, 1], ALU.add).then_inc(sq_summed, 1)
                gate_mul(g, 0)
                gate_mul(g, 1)
                gated_y(g, 0)
                gated_y(g, 1)
                gate_mul(g, 2)
                gated_y(g, 2)
                merge(g, 2)
                gate_mul(g, 3)
                gated_y(g, 3)
                merge(g, 3)

            with pool.Fori(0, 7) as r:
                for q in range(3):
                    pool.wait_ge(gate_made, r * 3 + q + 1)
                    pool.wait_ge(conv_made, r * 6 + 2 * q + 2)
                    pool.tensor_tensor(prod[:, bass.ds(r * 3 + q, 1), :].rearrange("p a t -> p (a t)"),
                                       conv[:, 2 * q], conv[:, 2 * q + 1], ALU.mult).then_inc(prod_made, 1)
            pool.wait_ge(gate_made, 22)
            pool.wait_ge(conv_made, 44)
            pool.tensor_tensor(prod[:, 21], conv[:, 0], conv[:, 1], ALU.mult).then_inc(prod_made, 1)

        @block.scalar
        def _(act):
            def split_hi(u, count, free):
                act.wait_ge(raw_in[raw_slot(u)], count)
                if free is not None:
                    act.wait_ge(proj_done, free)
                act.activation(w_hi[:, slot(u)].rearrange("p k c -> p (k c)"),
                               raw[:, raw_slot(u)].rearrange("p k c -> p (k c)"), ACT.Copy).then_inc(hi_made, 1)

            def split_hi_g(g, n):
                u = U_MIX + n
                free = u - 5
                if 6 <= n < 10:
                    free = U_MIX + 4
                split_hi(u, (g * (NU // RAW) + raw_count(u)) * 16, g * NU + free)

            act.dma_start(x_tok[:], x[0].rearrange("(t p) d -> p t d", p=P)).then_inc(x_in, 16)
            act.wait_ge(vecs_made, 3)
            act.activation(c_act, vecs[:, V_C:V_C + 8], ACT.Sigmoid).then_inc(start_act, 1)
            act.wait_ge(start_dve, 3)
            act.activation(lbt[:, 1:3].rearrange("p a k -> p (a k)"), lbt[:, 1:3].rearrange("p a k -> p (a k)"),
                           ACT.Exp).then_inc(start_act, 1)
            act.wait_ge(x_in, 16)
            for t in range(TT):
                act.activation(xn_tok[:, t], x_tok[:, t], ACT.Square, accum_out=ssq[:, t:t + 1]).then_inc(start_act, 1)
            act.wait_ge(start_dve, 12)
            act.activation(rst[:, :], rst[:, :], ACT.Sqrt).then_inc(start_act, 1)
            act.wait_ge(start_act, 7)
            for t in range(TT):
                act.activation(xn_tok[:, t], x_tok[:, t], ACT.Copy, scale=rst[:, t:t + 1]).then_inc(start_act, 1)
            for k in range(KT):
                act.wait_ge(x_turned, 2 * k + 2)
                act.activation(xnT[:, k], ps[:, 2 * (k % 2) + 3], ACT.Copy).then_inc(xnT_made, 1)
            split_hi(0, 16, None)
            act.wait_ge(ada0_made, 2)
            for k in range(KT):
                act.wait_ge(xnT_made, k + 1)
                act.activation(h_hi[:, k], xnT[:, k], ACT.Identity, bias=ada[:, k:k + 1],
                               scale=a_mix[:, k:k + 1]).then_inc(h_hi_made, 1)
            for n in range(AHEAD):
                split_hi(U_MIX + n, 16 * raw_count(U_MIX + n), None)
            act.wait_ge(proj_done, 1)
            act.wait_ge(xT_out, 16)
            act.activation(lrT[:, :], ps[0:LOWRANK, B_PROJ], ACT.Copy).then_inc(taken_act, 1)

            def exps(g, h, inv):
                s = h % 2
                act.wait_ge(d_made, g * 6 + 2 * h + 2)
                if h == 2:
                    act.wait_ge(o_done, g * 4 + 2)
                act.activation(kp[:, s], d_last[:, s], ACT.Exp, scale=-inv).then_inc(exp_made, 1)
                act.activation(decay[:, h], bcum[:, s, CHUNK - 1::CHUNK], ACT.Exp, scale=inv).then_inc(exp_made, 1)
                act.activation(ks[:, s], d_ref[:, s], ACT.Exp, scale=-inv).then_inc(exp_made, 1)
                act.activation(qs[:, s], d_ref[:, s], ACT.Exp, scale=inv).then_inc(exp_made, 1)
                act.activation(qe[:, s], bcum[:, s], ACT.Exp, scale=inv).then_inc(exp_made, 1)

            def take_kT(g, h, u_free):
                act.wait_ge(turned, g * 3 + h + 1)
                act.wait_ge(u_done, g * 4 + u_free)
                act.activation(kT[:].rearrange("p t c -> p (t c)"), ps[:, MISC_T[h]], ACT.Copy).then_inc(kT_made, 1)

            def take_o(g, w, nw):
                act.wait_ge(o_done, g * 4 + w + 1)
                act.wait_ge(y_made, g * 4 + max(w - 1, 0))
                act.wait_ge(ss_done, g * 3 + w // 2)
                act.activation(sq[:, w % 2], ps[:, B_O + w % 2], ACT.Square).then_inc(sq_made, 1)
                act.activation(oe[:, w % 2], ps[:, B_O + w % 2], ACT.Copy, scale=nw).then_inc(o_taken, 1)

            def root(g, i, bank, dv):
                act.wait_ge(ss_done, g * 3 + i + 1)
                act.wait_ge(normed, g * 4 + (0, 2, 3)[i])
                act.activation(rn[:], ps[:, bank], ACT.Ln, bias=eps_c, scale=SCALE2 / dv).then_inc(ss_taken, 1)
                act.wait_ge(ss_taken, g * 3 + i + 1)
                act.activation(rn[:], rn[:], ACT.Exp, scale=-0.5).then_inc(rn_made, 1)

            with act.Fori(0, GROUPS) as g:
                for n in range(NU):
                    if n in (0, 1) or n >= 5:
                        split_hi_g(g, n + AHEAD)
                    if n == 4:
                        for m in (6, 7, 8):
                            split_hi_g(g, m)
                    if n == 10:
                        exps(g, 1, 1.0)
                    if n == 11:
                        exps(g, 2, 1.0)
                    act.wait_ge(proj_done, g * NU + n + 2)
                    bank = ps[:, B_PROJ + (U_MIX + n) % 2]
                    if n < 4:
                        act.activation(v[:, n], bank, ACT.Copy).then_inc(taken_act, 1)
                    if n == 4:
                        act.wait_ge(qq_made, g * 6)
                        act.activation(qry[:, 1], bank, ACT.Copy).then_inc(taken_act, 1)
                    if n == 5:
                        act.activation(key[:, 1], bank, ACT.Copy).then_inc(taken_act, 1)
                    if n in (6, 7):
                        i = n - 6
                        if i == 0:
                            act.wait_ge(la_made, g + 1)
                            act.wait_ge(scan_made, g * 3 + 1)
                        else:
                            act.wait_ge(kk_made, g * 6 + 2)
                        act.activation(lg[:, i], bank, ACT.Sigmoid).then_inc(sig_made, 1)
                        act.activation(key[:, i], bank, ACT.Sigmoid, scale=-1.0).then_inc(taken_act, 1)
                    if n in (8, 9):
                        i = n - 8
                        act.wait_ge(qq_made, g * 6 + 2)
                        act.activation(qry[:, i], bank, ACT.Sigmoid).then_inc(sig_made, 1)
                    if n in (10, 12, 14, 16):
                        w = (n - 10) // 2
                        act.wait_ge(merged_made, g * 2)
                        act.activation(gate[:, w], bank, ACT.Sigmoid).then_inc(sig_made, 1)
                    if n in (11, 13, 15, 17):
                        w = (n - 11) // 2
                        act.wait_ge(gated, g * 4 + w)
                        act.activation(gmul[:], bank, ACT.Sigmoid).then_inc(taken_act, 1)
                    if n == 3:
                        act.wait_ge(z_made, g + 1)
                        act.activation(lg[:, 1], lg[:, 0], ACT.Abs).then_inc(soft_step, 1)
                        act.wait_ge(soft_step, g * 3 + 1)
                        act.activation(lg[:, 1], lg[:, 1], ACT.Exp, scale=-1.0).then_inc(soft_step, 1)
                        act.wait_ge(soft_step, g * 3 + 2)
                        act.activation(lg[:, 1], lg[:, 1], ACT.Ln, bias=one_c).then_inc(soft_step, 1)
                    if n == 5:
                        exps(g, 0, 1.0 / LOGIT_NORM)
                    if n == 8:
                        take_kT(g, 0, 0)
                    if n == 9:
                        for i in range(2):
                            act.wait_ge(sig_made, g * 8 + i + 1)
                            act.activation(lg[:, i], lg[:, i], ACT.Ln, bias=lb[:, bass.ds(g * 2 + i, 1)],
                                           scale=omlb[:, bass.ds(g * 2 + i, 1)]).then_inc(ln_made, 1)
                    if n == 10:
                        take_o(g, 0, gnw[:, 0:1])
                    if n == 11:
                        take_o(g, 1, gnw[:, 1:2])
                    if n == 12:
                        take_kT(g, 1, 2)
                        root(g, 0, MISC_SS[0], GLA_DV)
                    if n == 14:
                        take_kT(g, 2, 3)
                        take_o(g, 2, hnw)
                    if n == 16:
                        take_o(g, 3, hnw)
                        root(g, 1, MISC_SS[1], HGRN_DV)
                    if n == 17:
                        root(g, 2, MISC_SS[2], HGRN_DV)

            act.wait_ge(proj_done, U_OUT)
            def split_u(u):
                split_hi(u, 16 * raw_count(u), u - 5)

            for k in range(KT):
                if k == 6:
                    split_u(U_OUT + 4)
                    split_u(U_OUT + 5)
                act.wait_ge(merged_made, k + 1)
                act.activation(h_hi[:, k], merged[:, k], ACT.Copy).then_inc(m_hi_made, 1)
            act.activation(cols[:, 62:63], one_c, ACT.Ln).then_inc(start_act, 1)
            for j in range(KT):
                if j >= 2:
                    split_u(U_OUT + j + AHEAD)
                act.wait_ge(hres_made, j + 1)
                if j >= 3:
                    act.wait_ge(sq2_summed, j - 2)
                act.activation(n_tmp[:, j % 2] if j else rn2[:], hres[:, j], ACT.Square).then_inc(sq2_made, 1)
                act.wait_ge(a_ffn_made, 1)
                act.activation(prod[:, KT + j], hres[:, j], ACT.Copy, scale=a_ffn[:, j:j + 1]).then_inc(ha_made, 1)
            act.wait_ge(ss2_done, 1)
            act.activation(rn2[:], ps[:, B_MISC], ACT.Ln, bias=eps_c, scale=1.0 / D).then_inc(rn2_step, 1)
            act.wait_ge(rn2_step, 1)
            act.activation(rn2[:], rn2[:], ACT.Exp, scale=-0.5).then_inc(rn2_step, 1)
            for k in range(KT):
                act.wait_ge(n_made, k + 1)
                act.activation(h_hi[:, k], n_tmp[:, k % 2], ACT.Identity, bias=ada[:, 24 + k:25 + k]
                               ).then_inc(n_hi_made, 1)
            split_u(U_UP + 4)
            split_u(U_UP + 5)

            def conv_unit(r, m):
                u = U_UP + m
                if not (isinstance(r, int) and m < 2):
                    split_hi(u + AHEAD, (r * 2 + raw_count(u + AHEAD)) * 16, r * 6 + u + AHEAD - 5)
                ch = r * 3 + (m // 2) + (m % 2) * FT
                act.wait_ge(proj_done, r * 6 + u + 1)
                act.activation(conv[:, m], ps[:, m], ACT.Identity, bias=vecs[:, bass.ds(ch + V_CONVB, 1)],
                               scale=vecs[:, bass.ds(ch + V_TAP2, 1)]).then_inc(conv_a, 1)

            def silu_unit(r, m):
                act.wait_ge(conv_made, r * 6 + m + 1)
                act.activation(conv[:, m], conv[:, m], ACT.Silu).then_inc(gate_made, 1)

            for m in range(6):
                conv_unit(0, m)
                if m % 2:
                    silu_unit(0, m - 1)
            with act.Fori(1, 7) as r:
                for m in range(6):
                    act.wait_ge(prod_made, r * 3 + m // 2 - 2)
                    conv_unit(r, m)
                    if m % 2:
                        silu_unit(r, m - 1)
            act.wait_ge(prod_made, 19)
            for m in range(2):
                u = U_UP + 42 + m
                split_hi(u + AHEAD, 16 * raw_count(u + AHEAD), u + AHEAD - 5)
                act.wait_ge(proj_done, u + 1)
                ch = 21 + m * FT
                act.activation(conv[:, m], ps[:, m], ACT.Identity, bias=vecs[:, V_CONVB + ch:V_CONVB + ch + 1],
                               scale=vecs[:, V_TAP2 + ch:V_TAP2 + ch + 1]).then_inc(conv_a, 1)
            act.wait_ge(conv_made, 43)
            act.activation(conv[:, 0], conv[:, 0], ACT.Silu).then_inc(gate_made, 1)

            def prod_hi(r, f, free):
                act.wait_ge(prod_made, r * 6 + f + 1)
                act.wait_ge(proj_done, free)
                act.activation(h_hi[:, f % 6], prod[:, bass.ds(r * 6 + f, 1), :].rearrange("p a t -> p (a t)"),
                               ACT.Copy).then_inc(p_hi_made, 1)

            for f in range(AHEAD):
                prod_hi(0, f, U_DOWN)
            with act.Fori(0, 3) as r:
                for m in range(6):
                    u = U_DOWN + m + AHEAD
                    split_hi(u, (r * 2 + raw_count(u)) * 16, r * 6 + u - 5)
                    prod_hi(r, m + AHEAD, r * 6 + max(u - 5, U_DOWN))
            act.activation(cols[:, 62:63], one_c, ACT.Sqrt).then_inc(start_act, 1)
            for t in range(TT):
                for half in range(2):
                    act.wait_ge(fin_step, 4 * t + 2 * half + 2)
                    act.activation(prod[:, half], hres_tok[:, t, half * T:(half + 1) * T], ACT.Square,
                                   accum_out=fss[:, 2 * t + half:2 * t + half + 1]).then_inc(fsq_made, 1)
                act.wait_ge(frs_made, 2 * t + 2)
                act.activation(frs[:, t:t + 1], frs[:, t:t + 1], ACT.Sqrt, scale=float(D)).then_inc(fsq_made, 1)

        @block.vector
        def _(dve):
            def split_lo(u, count):
                dve.wait_ge(hi_made, count)
                dve.tensor_tensor(w_lo[:, slot(u)].rearrange("p k c -> p (k c)"),
                                  raw[:, raw_slot(u)].rearrange("p k c -> p (k c)"),
                                  w_hi[:, slot(u)].rearrange("p k c -> p (k c)").bitcast(F32),
                                  ALU.subtract).then_inc(lo_made, 1)

            dve.memset(rows[:], 0.0).then_inc(rows_zero, 1)
            dve.memset(cols[:, 0:1], EPS).then_inc(cols_made, 1)
            dve.memset(cols[:, 1:2], 1.0).then_inc(cols_made, 1)
            dve.memset(qscale, float(SCALE2) ** 0.5).then_inc(cols_made, 1)
            for i in range(3):
                dve.wait_ge(vecs_turned, 3)
                dve.tensor_copy(vecs[:, i * P:(i + 1) * P], ps[:, 0, i * P:(i + 1) * P]).then_inc(vecs_made, 1)
            dve.wait_ge(vecs_made, 3)
            l0, l1 = vecs[:, V_LB:V_LB + 8], vecs[:, V_LB + 8:V_LB + 16]
            dve.tensor_tensor(lbt[:, 0], l0, l1, ALU.max).then_inc(start_dve, 1)
            dve.wait_ge(start_dve, 1)
            dve.tensor_tensor(lbt[:, 1], l0, lbt[:, 0], ALU.subtract).then_inc(start_dve, 1)
            dve.tensor_tensor(lbt[:, 2], l1, lbt[:, 0], ALU.subtract).then_inc(start_dve, 1)
            dve.wait_ge(start_act, 1)
            dve.tensor_tensor(c_act, c_act, vecs[:, V_C:V_C + 8], ALU.mult).then_inc(start_dve, 1)
            dve.wait_ge(start_act, 2)
            dve.tensor_tensor(lbt[:, 3], lbt[:, 1], lbt[:, 2], ALU.add).then_inc(start_dve, 1)
            dve.wait_ge(start_dve, 5)
            dve.reciprocal(lbt[:, 4], lbt[:, 3]).then_inc(start_dve, 1)
            dve.wait_ge(start_dve, 6)
            dve.tensor_tensor(lb, lbt[:, 1], lbt[:, 4], ALU.mult).then_inc(start_dve, 1)
            dve.wait_ge(start_dve, 7)
            dve.tensor_scalar(omlb, lb, -1.0, 1.0, ALU.mult, ALU.add).then_inc(start_dve, 1)
            dve.wait_ge(cols_made, 3)
            dve.tensor_scalar(gnw, vecs[:, V_GNW:V_GNW + 2], qscale, None, ALU.mult).then_inc(start_dve, 1)
            dve.tensor_scalar(hnw, vecs[:, V_HNW:V_HNW + 1], qscale, None, ALU.mult).then_inc(start_dve, 1)

            def ada0_rows(k):
                dve.wait_ge(ada0_in[k % 4], 16 * (k // 4 + 1))
                if k == 0:
                    ins = dve.tensor_scalar(ada_acc0[:], ada_w0[:, 0], c_act[:, 0:1], None, ALU.mult)
                else:
                    dve.wait_ge(ada0_used, k)
                    ins = dve.scalar_tensor_tensor(out=ada_acc0[:], in0=ada_w0[:, k % 4], scalar=c_act[:, k:k + 1],
                                                   in1=ada_acc0[:], op0=ALU.mult, op1=ALU.add)
                ins.then_inc(ada0_used, 1)

            for k in range(KT):
                ada0_rows(k)
                if k == 2:
                    dve.wait_ge(start_act, 6)
                    dve.tensor_scalar(rst, ssq, 1.0 / D, EPS, ALU.mult, ALU.add).then_inc(start_dve, 1)
                    dve.wait_ge(start_dve, 11)
                    dve.reciprocal(rst, rst).then_inc(start_dve, 1)
                if k >= 4:
                    for j in (2 * k - 8, 2 * k - 7):
                        dve.wait_ge(x_turned, 2 * j + 1)
                        dve.tensor_copy(xT[:, j], ps[:, 2 * (j % 2) + 2]).then_inc(xT_made, 1)
            dve.wait_ge(ada0_summed, 1)
            dve.tensor_tensor(ada[:, 0:16], ps[:, 6, 0:16], vecs[:, V_BADA:V_BADA + 16], ALU.add).then_inc(ada0_made, 1)
            dve.wait_ge(ada0_made, 1)
            dve.scalar_tensor_tensor(out=a_mix, in0=ada[:, 8:16], scalar=1.0, in1=vecs[:, V_NMIX:V_NMIX + 8],
                                     op0=ALU.add, op1=ALU.mult).then_inc(ada0_made, 1)
            dve.wait_ge(ada0_made, 2)
            split_lo(0, 1)
            for k in range(KT):
                dve.wait_ge(xnT_made, k + 1)
                dve.tensor_scalar(h_tmp[:, k % 2], xnT[:, k], a_mix[:, k:k + 1], ada[:, k:k + 1],
                                  ALU.mult, ALU.add).then_inc(h_tmp_made, 1)
                dve.wait_ge(h_tmp_made, k + 1)
                dve.wait_ge(h_hi_made, k + 1)
                dve.tensor_tensor(h_lo[:, k], h_tmp[:, k % 2], h_hi[:, k].bitcast(F32), ALU.subtract
                                  ).then_inc(h_lo_made, 1)
            for n in range(AHEAD):
                split_lo(U_MIX + n, U_MIX + n + 1)
            dve.wait_ge(xT_out, 16)
            dve.wait_ge(mask_made, 6)
            dve.wait_ge(gk2_in, 16)

            def decays(g, h, b):
                b3 = bcum[:, b].rearrange("p (c t) -> p c t", t=CHUNK)
                if h:
                    dve.wait_ge(ln_made, g * 2 + h)
                dve.wait_ge(exp_made, g * 15 + (0, 0, 5)[h])
                src = lg[:, max(h - 1, 0)]
                dve.tensor_tensor_scan(bcum[:, b], scan_mask[:], src, 0.0, ALU.mult, ALU.add).then_inc(scan_made, 1)
                dve.wait_ge(scan_made, g * 3 + h + 1)
                for dst, at in ((d_last, CHUNK - 1), (d_ref, CHUNK // 2 - 1)):
                    dve.tensor_tensor(dst[:, b].rearrange("p (c t) -> p c t", t=CHUNK), b3,
                                      b3[:, :, at:at + 1].to_broadcast([P, NCH, CHUNK]),
                                      ALU.subtract).then_inc(d_made, 1)

            def times_k(g, h):
                s = h % 2
                for i, e in enumerate((kp, ks)):
                    dve.wait_ge(exp_made, g * 15 + 5 * h + (1, 3)[i])
                    if h == 0:
                        ins = dve.tensor_tensor(e[:, s], e[:, s], key[:, 1], ALU.mult)
                    else:
                        ins = dve.scalar_tensor_tensor(out=e[:, s], in0=key[:, h - 1],
                                                       scalar=omlb[:, bass.ds(g * 2 + (h - 1), 1)], in1=e[:, s],
                                                       op0=ALU.mult, op1=ALU.mult)
                    ins.then_inc(kk_made, 1)

            def mask_scores(g, h):
                dve.wait_ge(scored, g * 3 + h + 1)
                dve.wait_ge(o_done, g * 4 + (0, 2, 3)[h])
                dve.memset(cols[:, 63:64], 0.0)
                dve.copy_predicated(sT[:], causal[:].bitcast(U32).unsqueeze(1).to_broadcast([P, TT, P]),
                                    ps[:, MISC_S[h]].rearrange("p (t i) -> p t i", i=P)).then_inc(sT_made, 1)

            def states(g, w, h):
                dve.wait_ge(o_done, g * 4 + w)
                for i in range(NCH - 1):
                    if i == 0:
                        dve.wait_ge(u_done, g * 4 + w + 1)
                    u = ps[:, B_STATE + i % 2, (i // 2) * P:(i // 2 + 1) * P]
                    if i == 0:
                        ins = dve.tensor_copy(state[:, 0], u)
                    else:
                        dve.wait_ge(state_made, g * 28 + 7 * w + i)
                        ins = dve.scalar_tensor_tensor(out=state[:, i], in0=state[:, i - 1],
                                                       scalar=decay[:, h, i:i + 1], in1=u,
                                                       op0=ALU.mult, op1=ALU.add)
                    ins.then_inc(state_made, 1)

            def silu(g, n, buf):
                dve.wait_ge(sig_made, g * 8 + (3, 4, 5, 6, 7, 8)[BY_DVE.index(n)])
                dve.tensor_tensor(buf, ps[:, B_PROJ + (U_MIX + n) % 2], buf, ALU.mult).then_inc(taken_dve, 1)

            def ada_rows(g, m):
                dve.wait_ge(ada_in[m % 2], (g * 4 + m // 2 + 1) * 16)
                if m == 0:
                    dve.wait_ge(ada_summed, g)
                    ins = dve.tensor_scalar(ada_acc[:], ada_w[:, 0], c_act[:, 0:1], None, ALU.mult)
                else:
                    dve.wait_ge(ada_used, g * KT + m)
                    ins = dve.scalar_tensor_tensor(out=ada_acc[:], in0=ada_w[:, m % 2], scalar=c_act[:, m:m + 1],
                                                   in1=ada_acc[:], op0=ALU.mult, op1=ALU.add)
                ins.then_inc(ada_used, 1)

            def norm(g, w, i):
                dve.wait_ge(rn_made, g * 3 + i + 1)
                dve.wait_ge(o_taken, g * 4 + w + 1)
                dve.tensor_tensor(oe[:, w % 2], oe[:, w % 2], rn[:], ALU.mult).then_inc(normed, 1)

            with dve.Fori(0, GROUPS) as g:
                dve.wait_ge(z_done, g)
                dve.tensor_copy(gk2[0:LOWRANK, 0:P], gk2[32:32 + LOWRANK, bass.ds(g * P, P)]).then_inc(gk2_made, 1)
                for n in range(NU):
                    ms = [n + AHEAD] if (n in (0, 1) or n >= 5) else ([6, 7, 8] if n == 4 else [])
                    for m in ms:
                        split_lo(U_MIX + m, g * NU + U_MIX + m + 1)
                    if 1 <= n < 9:
                        ada_rows(g, n - 1)
                    if n == 3:
                        dve.wait_ge(z_done, g + 1)
                        dve.tensor_scalar(lg[:, 0], ps[:, MISC_Z], vecs[:, bass.ds(g + V_BGK, 1)], None, ALU.add
                                          ).then_inc(z_made, 1)
                        dve.wait_ge(soft_step, g * 3 + 3)
                        dve.scalar_tensor_tensor(out=lg[:, 0], in0=lg[:, 0], scalar=0.0, in1=lg[:, 1],
                                                 op0=ALU.min, op1=ALU.subtract).then_inc(la_made, 1)
                        dve.wait_ge(la_made, g + 1)
                        decays(g, 0, 0)
                    if n == 5:
                        dve.wait_ge(taken_act, g * N_ACT + taken_counts(5)[1] + 1)
                        times_k(g, 0)
                    if n == 6:
                        mask_scores(g, 0)
                    if n == 8:
                        silu(g, 8, qry[:, 0])
                        states(g, 0, 0)
                    if n == 9:
                        silu(g, 9, qry[:, 1])
                        decays(g, 1, 1)
                        states(g, 1, 0)
                        decays(g, 2, 0)
                    if n == 10:
                        times_k(g, 1)
                        silu(g, 10, gate[:, 0])
                    if n == 11:
                        times_k(g, 2)
                        mask_scores(g, 1)
                    if n == 12:
                        silu(g, 12, gate[:, 1])
                        states(g, 2, 1)
                    if n == 13:
                        norm(g, 0, 0)
                        norm(g, 1, 0)
                    if n == 14:
                        mask_scores(g, 2)
                        silu(g, 14, gate[:, 2])
                        states(g, 3, 2)
                    if n == 16:
                        silu(g, 16, gate[:, 3])
                        norm(g, 2, 1)
                    if n == 17:
                        dve.wait_ge(ada_summed, g + 1)
                        dve.tensor_tensor(ada[:, bass.ds(g * 8 + 16, 8)], ps[:, B_STATE + 1, 3 * P:3 * P + 8],
                                          vecs[:, bass.ds(g * 8 + V_BADA + 16, 8)], ALU.add).then_inc(ada_made, 1)
                        norm(g, 3, 2)

            for k in range(KT):
                if k == 6:
                    split_lo(U_OUT + 4, U_OUT + 5)
                    split_lo(U_OUT + 5, U_OUT + 6)
                dve.wait_ge(m_hi_made, k + 1)
                dve.tensor_tensor(h_lo[:, k], merged[:, k], h_hi[:, k].bitcast(F32), ALU.subtract).then_inc(m_lo_made, 1)
            dve.wait_ge(ada_made, GROUPS)
            dve.scalar_tensor_tensor(out=a_ffn, in0=ada[:, 32:40], scalar=1.0, in1=vecs[:, V_NFFN:V_NFFN + 8],
                                     op0=ALU.add, op1=ALU.mult).then_inc(a_ffn_made, 1)
            dve.wait_ge(const_made, 3)
            dve.wait_ge(m_lo_made, KT)
            for j in range(KT):
                dve.tensor_scalar(prod[:, j // 4, (j % 4) * P:(j % 4 + 1) * P], ident[:], ada[:, 40 + j:41 + j], None,
                                  ALU.mult).then_inc(diag_made, 1)
            dve.wait_ge(xT_back, 16)
            for j in range(KT):
                if j >= 2:
                    split_lo(U_OUT + j + AHEAD, U_OUT + j + AHEAD + 1)
                dve.wait_ge(proj_done, U_OUT + max(j, 3) + 1)
                dve.scalar_tensor_tensor(out=hres[:, j], in0=ps[:, OUT_BANKS[j % 4]],
                                         scalar=ada[:, 16 + j:17 + j], in1=hres[:, j],
                                         op0=ALU.mult, op1=ALU.add).then_inc(hres_made, 1)
                if j:
                    dve.wait_ge(sq2_made, j + 1)
                    if j >= 2:
                        dve.wait_ge(sq2_summed, j - 1)
                    dve.tensor_tensor(rn2[:], rn2[:], n_tmp[:, j % 2], ALU.add).then_inc(sq2_summed, 1)
            dve.wait_ge(gf_done, 1)
            dve.tensor_copy(gf_b[:].rearrange("p (a b) -> p a b", a=2), ps[:, B_O:B_O + 2]).then_inc(gf_made, 1)

            def take_token_major(t):
                dve.wait_ge(ht_done, t + 1)
                dve.tensor_copy(hres_tok[:, t].rearrange("p (a b) -> p a b", a=2),
                                ps[:, B_O - 2 * (t % 2):B_O - 2 * (t % 2) + 2]).then_inc(ht_made, 1)

            for t in range(TT - 1):
                take_token_major(t)
            dve.wait_ge(rn2_step, 2)
            dve.wait_ge(ha_made, KT)
            for k in range(KT):
                if k >= 2:
                    dve.wait_ge(n_hi_made, k - 1)
                dve.tensor_tensor(n_tmp[:, k % 2], prod[:, KT + k], rn2[:], ALU.mult).then_inc(n_made, 1)
                dve.wait_ge(n_made, k + 1)
                dve.wait_ge(n_hi_made, k + 1)
                dve.scalar_tensor_tensor(out=h_lo[:, k], in0=n_tmp[:, k % 2], scalar=ada[:, 24 + k:25 + k],
                                         in1=h_hi[:, k].bitcast(F32), op0=ALU.add, op1=ALU.subtract
                                         ).then_inc(n_lo_made, 1)
                if k == 0:
                    take_token_major(TT - 1)
            split_lo(U_UP + 4, U_UP + 5)
            split_lo(U_UP + 5, U_UP + 6)

            def taps(r, m, b, end):
                ch = r * 3 + (m // 2) + (m % 2) * FT if end is None else end + (m % 2) * FT
                dve.wait_ge(conv_a, r * 6 + b + 1)
                dve.scalar_tensor_tensor(out=conv[:, m, 1:T], in0=ps[:, m, 0:T - 1],
                                         scalar=vecs[:, bass.ds(ch + V_TAP1, 1)], in1=conv[:, m, 1:T],
                                         op0=ALU.mult, op1=ALU.add).then_inc(conv_b_, 1)
                dve.wait_ge(conv_b_, r * 6 + b + 1)
                dve.scalar_tensor_tensor(out=conv[:, m, 2:T], in0=ps[:, m, 0:T - 2],
                                         scalar=vecs[:, bass.ds(ch + V_TAP0, 1)], in1=conv[:, m, 2:T],
                                         op0=ALU.mult, op1=ALU.add).then_inc(conv_made, 1)

            def up_round(r, first):
                for m in range(6):
                    u = U_UP + m + AHEAD
                    if not (first and m < 2):
                        split_lo(u, r * 6 + u + 1)
                    taps(r, m, m, None)

            up_round(0, True)
            with dve.Fori(1, 7) as r:
                up_round(r, False)
            for m in range(2):
                u = U_UP + 42 + m + AHEAD
                split_lo(u, u + 1)
                taps(0, m, 42 + m, 21)

            def prod_lo(r, f):
                dve.wait_ge(p_hi_made, r * 6 + f + 1)
                dve.tensor_tensor(h_lo[:, f % 6], prod[:, bass.ds(r * 6 + f, 1), :].rearrange("p a t -> p (a t)"),
                                  h_hi[:, f % 6].bitcast(F32), ALU.subtract).then_inc(p_lo_made, 1)

            for f in range(AHEAD):
                prod_lo(0, f)
            with dve.Fori(0, 3) as r:
                for m in range(6):
                    u = U_DOWN + m + AHEAD
                    split_lo(u, r * 6 + u + 1)
                    prod_lo(r, m + AHEAD)
            dve.wait_ge(gf_made, 1)
            dve.wait_ge(fw_in, 16)
            dve.wait_ge(ht_made, TT)
            for t in range(TT):
                for half in range(2):
                    d = slice(half * T, (half + 1) * T)
                    y = prod[:, 2 + half]
                    i = 4 * t + 2 * half
                    dve.wait_ge(y_done, 2 * t + half + 1)
                    dve.tensor_tensor(y, ps[:, 2 * t + half], gf_b[:, d], ALU.mult).then_inc(fin_step, 1)
                    dve.wait_ge(fin_step, i + 1)
                    dve.tensor_tensor(hres_tok[:, t, d], hres_tok[:, t, d], y, ALU.add).then_inc(fin_step, 1)
                dve.wait_ge(fsq_made, 3 * t + 2)
                dve.tensor_scalar(frs[:, t:t + 1], fss[:, 2 * t:2 * t + 1], fss[:, 2 * t + 1:2 * t + 2], EPS * D,
                                  ALU.add, ALU.add).then_inc(frs_made, 1)
                dve.wait_ge(frs_made, 2 * t + 1)
                dve.reciprocal(frs[:, t:t + 1], frs[:, t:t + 1]).then_inc(frs_made, 1)
                dve.wait_ge(fsq_made, 3 * t + 3)
                for half in range(2):
                    d = slice(half * T, (half + 1) * T)
                    dve.scalar_tensor_tensor(out=hres_tok[:, t, d], in0=hres_tok[:, t, d], scalar=frs[:, t:t + 1],
                                             in1=fw_b[:, d], op0=ALU.mult, op1=ALU.mult).then_inc(fin_made, 1)

        @block.tensor
        def _(pe):
            def three(dst, pairs, start=True, stop=True):
                n = len(pairs)
                for i, ((a_hi, a_lo), (b_hi, b_lo)) in enumerate(pairs):
                    pe.matmul(dst, a_hi, b_hi, start=start and i == 0, stop=False)
                    pe.matmul(dst, a_hi, b_lo, start=False, stop=False)
                    last = pe.matmul(dst, a_lo, b_hi, start=False, stop=stop and i == n - 1)
                return last

            def unit(u, bank):
                s = slot(u)
                return three(ps[:, bank], [((w_hi[:, s, k], w_lo[:, s, k]), (h_hi[:, k], h_lo[:, k]))
                                           for k in range(KT)])

            pe.wait_ge(rows_in, 16 * 11)
            pe.wait_ge(const_made, 3)
            for i in range(3):
                pe.transpose(ps[:, 0, i * P:(i + 1) * P], rows[:, i], ident[:]).then_inc(vecs_turned, 1)
            pe.wait_ge(x_in, 16)
            pe.wait_ge(start_act, 11)
            for k in range(KT):
                if k >= 2:
                    pe.wait_ge(xT_made, k - 1)
                    pe.wait_ge(xnT_made, k - 1)
                for i, src in enumerate((x_tok, xn_tok)):
                    for t in range(TT):
                        last = pe.transpose(ps[:, 2 + 2 * (k % 2) + i, t * P:(t + 1) * P],
                                            src[:, t, k * P:(k + 1) * P], ident[:])
                    last.then_inc(x_turned, 1)
            pe.wait_ge(ada0_used, KT)
            for m in range(16):
                last = pe.matmul(ps[:, 6, m:m + 1], ada_acc0[:, m * P:(m + 1) * P], ones[:, 0:1],
                                 start=True, stop=True)
            last.then_inc(ada0_summed, 1)
            pe.wait_ge(vecs_made, 3)
            pe.wait_ge(lo_made, 1)
            for k in range(KT):
                pe.wait_ge(h_lo_made, k + 1)
                last = three(ps[:, B_PROJ], [((w_hi[:, slot(0), k], w_lo[:, slot(0), k]), (h_hi[:, k], h_lo[:, k]))],
                             start=k == 0, stop=k == KT - 1)
            last.then_inc(proj_done, 1)

            def turn(g, h):
                pe.wait_ge(kk_made, g * 6 + 2 * h + 1)
                for t in range(TT):
                    last = pe.transpose(ps[:, MISC_T[h], t * P:(t + 1) * P], kp[:, h % 2, t * P:(t + 1) * P], ident[:])
                last.then_inc(turned, 1)

            def score(g, h):
                pe.wait_ge(kk_made, g * 6 + 2 * h + 2)
                pe.wait_ge(qq_made, g * 6 + 2 * h + 1)
                half = CHUNK // 2
                for t in range(TT):
                    for j in range(0, P, half):
                        i = slice(t * P + j, t * P + (j // CHUNK + 1) * CHUNK)
                        last = pe.matmul(ps[j:j + half, MISC_S[h], i], ks[:, h % 2, t * P + j:t * P + j + half],
                                         qs[:, h % 2, i], start=True, stop=True)
                last.then_inc(scored, 1)

            def chunk_states(g, w, h):
                pe.wait_ge(kT_made, g * 3 + h + 1)
                pe.wait_ge(state_made, g * 28 + 7 * w)
                for i in range(NCH - 1):
                    if w == 0 and i == 1:
                        pe.wait_ge(ada_made, g)
                    rows_ = slice(CHUNK * (i % 2), CHUNK * (i % 2) + CHUNK)
                    last = pe.matmul(ps[:, B_STATE + i % 2, (i // 2) * P:(i // 2 + 1) * P], kT[rows_, i // 2],
                                     v[rows_, i // 2, w * P:(w + 1) * P], start=True, stop=True)
                last.then_inc(u_done, 1)

            def outputs(g, w, h):
                pe.wait_ge(sT_made, g * 3 + h + 1)
                pe.wait_ge(qq_made, g * 6 + 2 * h + 2)
                pe.wait_ge(o_taken, g * 4 + max(w - 1, 0))
                for t in range(TT):
                    o = ps[:, B_O + w % 2, t * P:(t + 1) * P]
                    pe.matmul(o, v[:, t, w * P:(w + 1) * P], sT[:, t], start=True, stop=False)
                    for i in (2 * t, 2 * t + 1):
                        if i:
                            pe.wait_ge(state_made, g * 28 + 7 * w + i)
                            last = pe.matmul(o[:, (i % 2) * CHUNK:(i % 2 + 1) * CHUNK], state[:, i - 1],
                                             qe[:, h % 2, i * CHUNK:(i + 1) * CHUNK], start=False, stop=i % 2 == 1)
                last.then_inc(o_done, 1)

            def square_sums(g, i, w):
                if i == 0:
                    pe.wait_ge(sq_summed, g + 1)
                else:
                    pe.wait_ge(sq_made, g * 4 + w + 1)
                pe.matmul(ps[:, MISC_SS[i]], ones[:], sq[:, w % 2], start=True, stop=True).then_inc(ss_done, 1)

            def group(g, first):
                for n in range(NU):
                    u = U_MIX + n
                    if n == 0:
                        pe.wait_ge(lo_made, g * NU + U_MIX + 4)
                    elif n >= 4:
                        pe.wait_ge(lo_made, g * NU + u + 1)
                    if not (first and n == 0):
                        if first and n == 1:
                            pe.wait_ge(taken_act, 1)
                        else:
                            prod_wait(pe, g, n)
                    bank = B_PROJ + u % 2
                    if n < 4:
                        tok = slice(n * P, (n + 1) * P)
                        last = three(ps[:, bank].rearrange("p (a b) -> p a b", b=P), [((h_hi[:, k, tok], h_lo[:, k, tok]),
                                                    (w_hi[:, 0:4, k], w_lo[:, 0:4, k])) for k in range(KT)])
                    else:
                        last = unit(u, bank)
                    last.then_inc(proj_done, 1)
                    if n == 2:
                        pe.wait_ge(gk2_made, g + 1)
                        pe.wait_ge(taken_act, g * N_ACT + 1)
                        pe.wait_ge(ss_taken, g * 3)
                        pe.matmul(ps[:, MISC_Z], gk2[0:LOWRANK, 0:P], lrT[:], start=True, stop=True).then_inc(z_done, 1)
                    if n == 6:
                        score(g, 0)
                    if n == 7:
                        pe.wait_ge(z_made, g + 1)
                        turn(g, 0)
                    if n == 8:
                        chunk_states(g, 0, 0)
                    if n == 9:
                        outputs(g, 0, 0)
                        chunk_states(g, 1, 0)
                    if n == 10:
                        outputs(g, 1, 0)
                    if n == 11:
                        pe.wait_ge(sT_made, g * 3 + 1)
                        turn(g, 1)
                        pe.wait_ge(kT_made, g * 3 + 1)
                        score(g, 1)
                    if n == 12:
                        chunk_states(g, 2, 1)
                        square_sums(g, 0, 0)
                    if n == 13:
                        outputs(g, 2, 1)
                        pe.wait_ge(sT_made, g * 3 + 2)
                        turn(g, 2)
                    if n == 14:
                        pe.wait_ge(ss_taken, g * 3 + 1)
                        score(g, 2)
                        chunk_states(g, 3, 2)
                    if n == 15:
                        outputs(g, 3, 2)
                        pe.wait_ge(kT_made, g * 3 + 3)
                        square_sums(g, 1, 2)
                    if n == 16:
                        pe.wait_ge(ada_used, g * KT + KT)
                        pe.wait_ge(state_made, g * 28 + 28)
                        for m in range(KT):
                            last = pe.matmul(ps[:, B_STATE + 1, 3 * P + m:3 * P + m + 1], ada_acc[:, m * P:(m + 1) * P],
                                             ones[:, 0:1], start=True, stop=True)
                        last.then_inc(ada_summed, 1)
                    if n == 17:
                        pe.wait_ge(sT_made, g * 3 + 3)
                        square_sums(g, 2, 3)

            group(0, True)
            with pe.Fori(1, GROUPS) as g:
                group(g, False)

            def interleaved(u0, banks, ready, step):
                pe.wait_ge(lo_made, u0 + 4)
                for k in range(KT):
                    pe.wait_ge(ready, step * (k + 1))
                    for i, bank in enumerate(banks):
                        s = slot(u0 + i)
                        last = three(ps[:, bank], [((w_hi[:, s, k], w_lo[:, s, k]), (h_hi[:, k], h_lo[:, k]))],
                                     start=k == 0, stop=k == KT - 1)
                        if k == KT - 1:
                            last.then_inc(proj_done, 1)

            pe.wait_ge(taken_act, GROUPS * N_ACT + 1)
            pe.wait_ge(taken_dve, GROUPS * N_DVE)
            pe.wait_ge(ada_made, GROUPS)
            interleaved(U_OUT, OUT_BANKS, m_lo_made, 1)
            for j in range(4, KT):
                pe.wait_ge(lo_made, U_OUT + j + 1)
                pe.wait_ge(hres_made, j - 3)
                unit(U_OUT + j, OUT_BANKS[j % 4]).then_inc(proj_done, 1)
            pe.wait_ge(diag_made, KT)
            pe.wait_ge(o_taken, 4 * GROUPS)
            for j in range(KT):
                last = pe.matmul(ps[:, B_O + j // 4, (j % 4) * P:(j % 4 + 1) * P], ones[:],
                                 prod[:, j // 4, (j % 4) * P:(j % 4 + 1) * P], start=True, stop=True)
            last.then_inc(gf_done, 1)

            def token_major(t):
                if t == 0:
                    pe.wait_ge(gf_made, 1)
                if t == 1:
                    pe.wait_ge(hres_made, KT)
                if t >= 2:
                    pe.wait_ge(ht_made, t - 1)
                for k in range(KT):
                    last = pe.transpose(ps[:, B_O - 2 * (t % 2) + k // 4, (k % 4) * P:(k % 4 + 1) * P],
                                        hres[:, k, t * P:(t + 1) * P], ident[:])
                last.then_inc(ht_done, 1)

            pe.wait_ge(sq2_summed, KT - 1)
            pe.wait_ge(ss_taken, 3 * GROUPS)
            pe.matmul(ps[:, B_MISC], ones[:], rn2[:], start=True, stop=True).then_inc(ss2_done, 1)
            for t in range(TT):
                token_major(t)

            def up_unit(r, m, b):
                pe.wait_ge(lo_made, r * 6 + U_UP + b + 1)
                return unit(U_UP + m, m)

            pe.wait_ge(rn2_step, 1)
            interleaved(U_UP, range(4), n_lo_made, 1)
            pe.wait_ge(ht_made, TT)
            for m in (4, 5):
                up_unit(0, m, m).then_inc(proj_done, 1)
            with pe.Fori(1, 7) as r:
                for m in range(6):
                    pe.wait_ge(conv_made, r * 6 + m - 5)
                    up_unit(r, m, m).then_inc(proj_done, 1)
            for m in range(2):
                pe.wait_ge(conv_made, 42 + m - 5)
                up_unit(0, m, 42 + m).then_inc(proj_done, 1)

            def down(f_slot, u, t, half, start=False, stop=False):
                s = slot(u)
                tok = slice(t * P, (t + 1) * P)
                cols_ = slice(4 * half, 4 * half + 4)
                return three(ps[:, 2 * t + half].rearrange("p (a b) -> p a b", b=P),
                             [((h_hi[:, f_slot, tok], h_lo[:, f_slot, tok]),
                               (w_hi[:, s, cols_], w_lo[:, s, cols_]))], start=start, stop=stop)

            def down_unit(f, start):
                for t in range(TT):
                    for half in range(2):
                        last = down(f % 6, U_DOWN + f, t, half, start=start)
                last.then_inc(proj_done, 1)

            pe.wait_ge(conv_made, 2 * FT)
            pe.wait_ge(ht_made, TT)
            pe.wait_ge(lo_made, U_DOWN + 1)
            pe.wait_ge(p_lo_made, 1)
            down_unit(0, True)
            with pe.Fori(0, 3) as r:
                for m in range(1, 7):
                    pe.wait_ge(lo_made, r * 6 + U_DOWN + m + 1)
                    pe.wait_ge(p_lo_made, r * 6 + m + 1)
                    down_unit(m, False)
            pe.wait_ge(lo_made, U_END)
            pe.wait_ge(p_lo_made, FT)
            for t in range(TT):
                for half in range(2):
                    for f in range(19, FT):
                        last = down(f % 6, U_DOWN + f, t, half, stop=f == FT - 1)
                    last.then_inc(y_done, 1)


_INS = ["x", "c", "w_ada", "b_ada", "norm_mix_w", "w_in", "w_gk2", "b_gk2", "gla_norm_w", "hgrn_lb",
        "hgrn_norm_w", "w_out", "norm_ffn_w", "w_up", "conv_w", "conv_b", "w_down", "final_norm_w"]


def kernel(**inputs):
    import numpy as np
    import concourse.bacc as bacc
    from concourse.bass_utils import run_bass_kernel_spmd as run

    nc = bacc.Bacc("TRN2", target_bir_lowering=False, num_devices=1)
    arrays, args = {}, []
    for name in _INS:
        a = np.ascontiguousarray(inputs[name])
        arrays[f"in_{name}_dram"] = a
        args.append(nc.dram_tensor(f"in_{name}_dram", a.shape, mybir.dt.from_np(a.dtype), kind="ExternalInput").ap())
    out = nc.dram_tensor("out_dram", (1, T, D), F32, kind="ExternalOutput").ap()
    build(nc, *args, out)
    r = run(nc, [arrays], core_ids=[0])
    return r.results[0]["out_dram"]
```

```python
from contextlib import ExitStack

import concourse.bass as bass
from concourse import mybir

F32 = mybir.dt.float32
F32R = mybir.dt.float32r
BF16 = mybir.dt.bfloat16
U32 = mybir.dt.uint32
ALU = mybir.AluOpType
ACT = mybir.ActivationFunctionType

P = 128
D = 1024
T = 512
KT = D // P
TT = T // P
CHUNK = 64
NCH = T // CHUNK
GROUPS = 4
D_FF = 2816
FT = D_FF // P
GLA_QK, GLA_V, LOWRANK = 512, 1024, 16
GLA_DV = GLA_V // GROUPS
HGRN_DV = 128
LOGIT_NORM = 16.0
SCALE2 = 1.0 / 128
EPS = 1e-6

GQ, GK, GV, GG = 0, GLA_QK, 2 * GLA_QK, 2 * GLA_QK + GLA_V
GLR = GG + GLA_V
HQ = GLR + LOWRANK
HF, HI, HG, MA, MB = (HQ + i * D for i in range(1, 6))
UNITS = [(GV, 256), (GV + P, 256), (HI, 256), (HI + P, 256), (GQ, P), (GK, P),
         (HF, 256), (HF + P, 256), (HQ, 256), (HQ + P, 256),
         (GG, 256), (MA, 256), (GG + P, 256), (MA + P, 256),
         (HG, 256), (MB, 256), (HG + P, 256), (MB + P, 256)]
NU = len(UNITS)
U_MIX = 1
U_OUT = U_MIX + GROUPS * NU
U_UP = U_OUT + KT
U_DOWN = U_UP + 2 * FT
U_END = U_DOWN + FT
RING, RAW = 6, 3
AHEAD = 4
BY_DVE = (8, 9, 10, 12, 14, 16)

B_PROJ, B_MISC, B_STATE, B_O = 0, 2, 4, 6
V_BANKS = (1, 0, 4, 5)
OUT_BANKS = (0, 1, 4, 5)
TAKE_AFTER = (0, 1, 3, 5)
MISC_Z = 2
MISC_T = (2, 3, 2)
MISC_S = (3, 2, 3)
MISC_SS = (3, 2, 3)

V_BADA, V_NMIX, V_NFFN, V_CONVB, V_LB, V_BGK = 0, 48, 56, 64, 108, 124
V_TAP0, V_TAP1, V_C, V_GNW, V_HNW, V_TAP2 = 128, 172, 216, 224, 226, 256


def slot(u):
    return (u + 5) % RING


def raw_slot(u):
    return (u + 2) % RAW


def raw_count(u):
    return u // RAW + 1


def taken_counts(n):
    if n in BY_DVE:
        return True, BY_DVE.index(n) + 1
    return False, len([m for m in range(n + 1) if m not in BY_DVE])


N_DVE = len(BY_DVE)
N_ACT = NU - N_DVE


def build(nc, x, c, w_ada, b_ada, norm_mix_w, w_in, w_gk2, b_gk2, gla_norm_w, hgrn_lb, hgrn_norm_w,
          w_out, norm_ffn_w, w_up, conv_w, conv_b, w_down, final_norm_w, out):
    ctx = ExitStack()
    with ctx:
        def sem(name):
            return ctx.enter_context(nc.semaphore(name))

        def sbuf(stack):
            def alloc(name, shape, dt=F32):
                return stack.enter_context(nc.sbuf_tensor(name, shape, dt))
            return alloc

        sb = sbuf(ctx)
        raw = sb("raw", [P, RAW, KT, P])
        w_hi = sb("w_hi", [P, RING, KT, P], F32R)
        w_lo = sb("w_lo", [P, RING, KT, P], F32R)
        h_hi = sb("h_hi", [P, KT, T], F32R)
        h_lo = sb("h_lo", [P, KT, T], F32R)
        vecs = sb("vecs", [P, 3 * P])
        ada = sb("ada", [P, 48])
        ident = sb("ident", [P, P])
        ones = sb("ones", [P, P])
        cols = sb("cols", [P, 64])
        eps_c, one_c = cols[:, 0:1], cols[:, 1:2]
        c_act = cols[:, 2:10]
        a_mix = cols[:, 10:18]
        lb, omlb = cols[:, 18:26], cols[:, 26:34]
        a_ffn = cols[:, 34:42]
        gnw, hnw = cols[:, 42:44], cols[:, 44:45]
        ssq, rst = cols[:, 45:49], cols[:, 49:53]
        qscale = cols[:, 53:54]
        frs = cols[:, 54:58]
        fss = sb("fss", [P, 2 * TT])
        lbt = sb("lbt", [P, 5, KT])
        lrT = sb("lrT", [LOWRANK, T])
        gk2 = sb("gk2", [32 + LOWRANK, T])
        scan_mask = sb("scan_mask", [P, T], BF16)
        causal = sb("causal", [P, P])

        init = ExitStack()
        si = sbuf(init)
        rows = si("rows", [P, 3, P])
        x_tok = si("x_tok", [P, TT, D])
        xn = si("xn", [P, KT, T])
        xT = si("xT", [P, KT, T])
        ada_w0 = si("ada_w0", [P, KT, D])
        ada_acc0 = si("ada_acc0", [P, 2, D])
        h_tmp = si("h_tmp", [P, 2, T])
        rb = si("rb", [P, T])
        init.close()

        mix = ExitStack()
        sm = sbuf(mix)
        merged = sm("merged", [P, KT, T])
        ada_w = sm("ada_w", [P, 2, D])
        ada_acc = sm("ada_acc", [P, D])
        v = sm("v", [P, TT, 4 * P])
        qs = sm("qs", [P, 2, T])
        ks = sm("ks", [P, 2, T])
        qe = sm("qe", [P, 2, T])
        kp = sm("kp", [P, 2, T])
        bcum = sm("bcum", [P, 2, T])
        d_ref = sm("d_ref", [P, 2, T])
        d_last = sm("d_last", [P, 2, T])
        lg = sm("lg", [P, 2, T])
        key = sm("key", [P, 2, T])
        qry = sm("qry", [P, 2, T])
        decay = sm("decay", [P, 3, NCH])
        kT = sm("kT", [P, TT, P])
        sT = sm("sT", [P, TT, P])
        state = sm("state", [P, NCH - 1, P])
        gate = sm("gate", [P, 4, T])
        gmul = sm("gmul", [P, T])
        sq = sm("sq", [P, 2, T])
        oe = sm("oe", [P, 2, T])
        rn = sm("rn", [P, T])
        mix.close()

        sf = sbuf(ctx)
        prod = sf("prod", [P, FT, T])
        hres = sf("hres", [P, KT, T])
        hres_tok = sf("hres_tok", [P, TT, D])
        conv = sf("conv", [P, 6, T])
        n_tmp = sf("n_tmp", [P, 2, T])
        rn2 = sf("rn2", [P, T])
        fw_b = sf("fw_b", [P, D])
        p0_hi = sf("p0_hi", [P, T], F32R)
        p0_lo = sf("p0_lo", [P, T], F32R)
        gf_b = sf("gf_b", [P, D])
        xT_dram = nc.dram_tensor("xT_saved_dram", [P, KT, T], F32, kind="Internal").ap()

        ps = ctx.enter_context(nc.psum_tensor("ps", [P, 8, T], F32))

        rows_zero = sem("rows_zero")
        rows_in = sem("rows_in")
        x_in = sem("x_in")
        gk2_in = sem("gk2_in")
        fw_in = sem("fw_in")
        ada0_in = [sem(f"ada0_in{i}") for i in range(KT)]
        ada_in = [sem(f"ada_in{i}") for i in range(2)]
        raw_in = [sem(f"raw_in{i}") for i in range(RAW)]
        xT_out = sem("xT_out")
        xT_back = sem("xT_back")
        out_done = sem("out_done")
        const_made = sem("const_made")
        cols_made = sem("cols_made")
        mask_made = sem("mask_made")
        vecs_turned = sem("vecs_turned")
        vecs_made = sem("vecs_made")
        start_act = sem("start_act")
        start_dve = sem("start_dve")
        x_turned = sem("x_turned")
        xT_made_act = sem("xT_made_act")
        xT_made_dve = sem("xT_made_dve")
        rdiag_made = sem("rdiag_made")
        rb_done = sem("rb_done")
        rb_made = sem("rb_made")
        xn_made = sem("xn_made")
        ada0_used = sem("ada0_used")
        ada0_summed = sem("ada0_summed")
        ada0_made = sem("ada0_made")
        ada_summed = sem("ada_summed")
        h_tmp_made = sem("h_tmp_made")
        h_hi_made = sem("h_hi_made")
        h_lo_made = sem("h_lo_made")
        hi_made = sem("hi_made")
        lo_made = sem("lo_made")
        proj_done = sem("proj_done")
        taken_act = sem("taken_act")
        taken_dve = sem("taken_dve")
        ada_used = sem("ada_used")
        ada_made = sem("ada_made")
        gk2_made = sem("gk2_made")
        z_done = sem("z_done")
        z_made = sem("z_made")
        soft_step = sem("soft_step")
        ln_made = sem("ln_made")
        sig_made = sem("sig_made")
        la_made = sem("la_made")
        scan_made = sem("scan_made")
        d_made = sem("d_made")
        exp_made = sem("exp_made")
        kk_made = sem("kk_made")
        qq_made = sem("qq_made")
        turned = sem("turned")
        kT_made = sem("kT_made")
        scored = sem("scored")
        sT_made = sem("sT_made")
        u_done = sem("u_done")
        state_made = sem("state_made")
        o_done = sem("o_done")
        o_taken = sem("o_taken")
        sq_made = sem("sq_made")
        sq_summed = sem("sq_summed")
        ss_done = sem("ss_done")
        ss_taken = sem("ss_taken")
        rn_made = sem("rn_made")
        normed = sem("normed")
        gated = sem("gated")
        y_made = sem("y_made")
        merged_made = sem("merged_made")
        m_hi_made = sem("m_hi_made")
        m_lo_made = sem("m_lo_made")
        hres_made = sem("hres_made")
        sq2_made = sem("sq2_made")
        sq2_summed = sem("sq2_summed")
        ss2_done = sem("ss2_done")
        ha_made = sem("ha_made")
        rn2_step = sem("rn2_step")
        a_ffn_made = sem("a_ffn_made")
        n_made = sem("n_made")
        n_hi_made = sem("n_hi_made")
        n_lo_made = sem("n_lo_made")
        diag_made = sem("diag_made")
        gf_done = sem("gf_done")
        gf_made = sem("gf_made")
        ht_done = sem("ht_done")
        ht_made = sem("ht_made")
        conv_a = sem("conv_a")
        conv_b_ = sem("conv_b_")
        conv_made = sem("conv_made")
        gate_made = sem("gate_made")
        prod_made = sem("prod_made")
        p_hi_made = sem("p_hi_made")
        p_lo_made = sem("p_lo_made")
        y_done = sem("y_done")
        fin_step = sem("fin_step")
        fsq_made = sem("fsq_made")
        frs_made = sem("frs_made")
        fin_scaled = sem("fin_scaled")
        fin_made = sem("fin_made")
        fin_last = sem("fin_last")

        def unit_view(w):
            return w[0].rearrange("(k p) c -> p k c", p=P)

        win_v, wout_v, wup_v, wada_v = map(unit_view, (w_in, w_out, w_up, w_ada))
        wdown_v = w_down[0].rearrange("(f p) n -> f p n", p=P)

        def prod_wait(eng, g, n):
            m = n - 2
            gg = g
            if m < 0:
                m, gg = m + NU, g - 1
            dve, k = taken_counts(m)
            if dve:
                eng.wait_ge(taken_dve, gg * N_DVE + k)
            else:
                eng.wait_ge(taken_act, gg * N_ACT + k + 1)

        block = ctx.enter_context(nc.Block())

        @block.sync
        def _(sp):
            sp.wait_ge(rows_zero, 1)
            def row(dst, src, n):
                sp.dma_start(rows[dst % P:dst % P + n, dst // P, :], src).then_inc(rows_in, 16)
            row(V_C, c[0].rearrange("(r p) -> r p", p=P), 8)
            row(V_BADA, b_ada[0].rearrange("(r p) -> r p", p=P), 48)
            row(V_NMIX, norm_mix_w[0].rearrange("(r p) -> r p", p=P), 8)
            row(V_NFFN, norm_ffn_w[0].rearrange("(r p) -> r p", p=P), 8)
            row(V_CONVB, conv_b[0].rearrange("(r p) -> r p", p=P), 44)
            row(V_LB, hgrn_lb.rearrange("a (r p) -> (a r) p", p=P), 16)
            row(V_BGK, b_gk2[0].rearrange("(r p) -> r p", p=P), 4)
            row(V_TAP0, conv_w[0, 0:2].rearrange("a (r p) -> (a r) p", p=P), 88)
            row(V_GNW, gla_norm_w[0].rearrange("(r p) -> r p", p=P), 2)
            row(V_HNW, hgrn_norm_w[0].rearrange("(r p) -> r p", p=P), 1)
            row(V_TAP2, conv_w[0, 2].rearrange("(r p) -> r p", p=P), 44)
            def ada0_load(q, k):
                if q:
                    sp.wait_ge(ada0_used, k + 1)
                sp.dma_start(ada_w0[:, k].rearrange("p (a d) -> p a d", a=2),
                             wada_v[:, k, 0:2 * D].rearrange("p (a d) -> p a d", a=2)[:, :, q * T:(q + 1) * T]
                             ).then_inc(ada0_in[k], 16)

            def first_load(u):
                if u >= RAW:
                    sp.wait_ge(lo_made, u - RAW + 1)
                c0 = UNITS[u - U_MIX][0] if u else GLR
                sp.dma_start(raw[:, raw_slot(u)], win_v[:, :, c0:c0 + P]).then_inc(raw_in[raw_slot(u)], 16)

            first_load(0)
            for k in range(KT):
                ada0_load(0, k)
                if k % 2:
                    first_load(k // 2 + 1)
            for k in range(KT):
                ada0_load(1, k)
            sp.wait_ge(xT_made_act, KT // 2)
            sp.wait_ge(xT_made_dve, KT // 2)
            sp.dma_start(xT_dram, xT[:]).then_inc(xT_out, 16)

            def load(u, src, free):
                sp.wait_ge(lo_made, free)
                sp.dma_start(raw[:, raw_slot(u)], src).then_inc(raw_in[raw_slot(u)], 16)

            def group_loads(g, first):
                for n in range(NU):
                    c0, step = UNITS[n]
                    u = U_MIX + n
                    if not (first and u < 5):
                        load(u, win_v[:, :, bass.ds(g * step + c0, P)], g * NU + u - RAW + 1)
                    m = n - (9 if first else 5)
                    if 0 <= m < 8:
                        if not (first and m < 2):
                            sp.wait_ge(ada_used, g * 8 + m - 1)
                        elif m == 0:
                            sp.wait_ge(xT_out, 16)
                            sp.wait_ge(proj_done, 1)
                        sp.dma_start(ada_w[:, m % 2], wada_v[:, m, bass.ds(g * D + 2 * D, D)]
                                     ).then_inc(ada_in[m % 2], 16)

            group_loads(0, True)
            with sp.Fori(1, GROUPS) as g:
                group_loads(g, False)
            for j in range(KT):
                load(U_OUT + j, wout_v[:, :, j * P:(j + 1) * P], U_OUT + j - RAW + 1)
                if j == 5:
                    sp.wait_ge(m_lo_made, KT)
                    sp.dma_start(hres[:], xT_dram).then_inc(xT_back, 16)
                    sp.dma_start(fw_b[:], final_norm_w.rearrange("(a d) -> a d", a=1).to_broadcast([P, D])
                                 ).then_inc(fw_in, 16)
            with sp.Fori(0, 7) as r:
                for m in range(6):
                    u = U_UP + m
                    load(u, wup_v[:, :, bass.ds(r * 3 * P + (m // 2) * P + (m % 2) * D_FF, P)],
                         r * 6 + u - RAW + 1)
            for m in range(2):
                u = U_UP + 42 + m
                load(u, wup_v[:, :, 21 * P + m * D_FF:22 * P + m * D_FF], u - RAW + 1)
            with sp.Fori(0, 3) as r:
                for m in range(6):
                    u = U_DOWN + m
                    load(u, wdown_v[bass.ds(r * 6 + m, 1)].rearrange("a p n -> (a p) n"), r * 6 + u - RAW + 1)
            for f in range(18, FT):
                u = U_DOWN + f
                load(u, wdown_v[f], u - RAW + 1)
            for t in range(TT - 1):
                sp.wait_ge(fin_made, t + 1)
                sp.dma_start(out[0, t * P:(t + 1) * P, :], hres_tok[:, t]).then_inc(out_done, 16)
            for half in range(2):
                sp.wait_ge(fin_last, half + 1)
                d = slice(half * T, (half + 1) * T)
                sp.dma_start(out[0, (TT - 1) * P:T, d], hres_tok[:, TT - 1, d]).then_inc(out_done, 16)
            sp.wait_ge(out_done, 16 * (TT + 1))

        @block.gpsimd
        def _(pool):
            pool.memset(ones[:], 1.0).then_inc(const_made, 1)
            pool.memset(ident[:], 0.0).then_inc(const_made, 1)
            pool.wait_ge(const_made, 2)
            pool.affine_select(out=ident[:], in_=ident[:], compare_op=ALU.not_equal, fill=1.0, base=0,
                               pattern=[[-1, P]], channel_multiplier=1).then_inc(const_made, 1)
            pool.dma_start(gk2[32:32 + LOWRANK, :], w_gk2[0]).then_inc(gk2_in, 16)
            pool.memset(scan_mask[:], 1.0).then_inc(mask_made, 1)
            pool.memset(causal[:], 1.0).then_inc(mask_made, 1)
            pool.wait_ge(mask_made, 2)
            pool.memset(scan_mask[:].rearrange("p (c t) -> p c t", t=CHUNK)[:, :, 0:1], 0.0).then_inc(mask_made, 1)
            pool.affine_select(out=causal[:], in_=causal[:], compare_op=ALU.is_ge, fill=0.0, base=0,
                               pattern=[[1, P]], channel_multiplier=-1).then_inc(mask_made, 1)
            pool.wait_ge(mask_made, 4)
            pool.memset(causal[0:CHUNK, CHUNK:P], 0.0).then_inc(mask_made, 1)
            pool.wait_ge(rb_made, 1)
            pool.wait_ge(start_act, 6)
            for k in range(KT):
                pool.wait_ge(xT_made_dve if k % 2 else xT_made_act, k // 2 + 1)
                pool.tensor_tensor(xn[:, k], xT[:, k], rb[:], ALU.mult).then_inc(xn_made, 1)
            pool.wait_ge(xT_out, 16)
            pool.wait_ge(proj_done, 1)
            pool.memset(sT[:], 0.0).then_inc(mask_made, 1)
            def times_q(g, h, q):
                s = h % 2
                pool.wait_ge(exp_made, g * 15 + 5 * h + 4)
                pool.tensor_tensor(qs[:, s], qs[:, s], q, ALU.mult).then_inc(qq_made, 1)
                pool.wait_ge(exp_made, g * 15 + 5 * h + 5)
                pool.tensor_tensor(qe[:, s], qe[:, s], q, ALU.mult).then_inc(qq_made, 1)

            def gate_mul(g, w):
                pool.wait_ge(taken_dve, g * N_DVE + taken_counts(10 + 2 * w)[1])
                pool.wait_ge(taken_act, g * N_ACT + taken_counts(11 + 2 * w)[1] + 1)
                pool.tensor_tensor(gate[:, w], gate[:, w], gmul[:], ALU.mult).then_inc(gated, 1)

            def gated_y(g, w):
                pool.wait_ge(gated, g * 4 + w + 1)
                pool.wait_ge(normed, g * 4 + w + 1)
                pool.tensor_tensor(gate[:, w], gate[:, w], oe[:, w % 2], ALU.mult).then_inc(y_made, 1)

            def merge(g, w):
                pool.wait_ge(y_made, g * 4 + w + 1)
                pool.tensor_tensor(merged[:, bass.ds(g * 2 + (w - 2), 1), :].rearrange("p a t -> p (a t)"),
                                   gate[:, w - 2], gate[:, w], ALU.add).then_inc(merged_made, 1)

            with pool.Fori(0, GROUPS) as g:
                pool.wait_ge(taken_act, g * N_ACT + taken_counts(5)[1] + 1)
                times_q(g, 0, qry[:, 1])
                pool.wait_ge(taken_dve, g * N_DVE + 1)
                times_q(g, 1, qry[:, 0])
                pool.wait_ge(taken_dve, g * N_DVE + 2)
                times_q(g, 2, qry[:, 1])
                pool.wait_ge(sq_made, g * 4 + 2)
                pool.tensor_tensor(sq[:, 0], sq[:, 0], sq[:, 1], ALU.add).then_inc(sq_summed, 1)
                gate_mul(g, 0)
                gate_mul(g, 1)
                gated_y(g, 0)
                gated_y(g, 1)
                gate_mul(g, 2)
                gated_y(g, 2)
                merge(g, 2)
                gate_mul(g, 3)
                gated_y(g, 3)
                merge(g, 3)

            with pool.Fori(0, 7) as r:
                for q in range(3):
                    pool.wait_ge(gate_made, r * 3 + q + 1)
                    pool.wait_ge(conv_made, r * 6 + 2 * q + 2)
                    pool.tensor_tensor(prod[:, bass.ds(r * 3 + q, 1), :].rearrange("p a t -> p (a t)"),
                                       conv[:, 2 * q], conv[:, 2 * q + 1], ALU.mult).then_inc(prod_made, 1)
            pool.wait_ge(gate_made, 22)
            pool.wait_ge(conv_made, 44)
            pool.tensor_tensor(prod[:, 21], conv[:, 0], conv[:, 1], ALU.mult).then_inc(prod_made, 1)
            pool.wait_ge(fw_in, 16)
            for t in range(TT - 1):
                pool.wait_ge(fin_scaled, t + 1)
                pool.tensor_tensor(hres_tok[:, t], hres_tok[:, t], fw_b[:], ALU.mult).then_inc(fin_made, 1)

        @block.scalar
        def _(act):
            def split_hi(u, count, free):
                act.wait_ge(raw_in[raw_slot(u)], count)
                if free is not None:
                    act.wait_ge(proj_done, free)
                act.activation(w_hi[:, slot(u)].rearrange("p k c -> p (k c)"),
                               raw[:, raw_slot(u)].rearrange("p k c -> p (k c)"), ACT.Copy).then_inc(hi_made, 1)

            def split_hi_g(g, n):
                u = U_MIX + n
                free = u - 5
                if 6 <= n < 10:
                    free = U_MIX + 4
                split_hi(u, (g * (NU // RAW) + raw_count(u)) * 16, g * NU + free)

            act.dma_start(x_tok[:], x[0].rearrange("(t p) d -> p t d", p=P)).then_inc(x_in, 16)
            act.wait_ge(cols_made, 3)
            act.activation(cols[:, 62:63], one_c, ACT.Sigmoid).then_inc(start_act, 1)
            act.wait_ge(vecs_made, 3)
            act.activation(c_act, vecs[:, V_C:V_C + 8], ACT.Sigmoid).then_inc(start_act, 1)
            act.wait_ge(x_in, 16)
            for t in range(TT):
                act.activation(xn[:, 2 * t:2 * t + 2].rearrange("p a b -> p (a b)"), x_tok[:, t], ACT.Square, accum_out=ssq[:, t:t + 1]).then_inc(start_act, 1)
            for k in range(0, KT, 2):
                act.wait_ge(x_turned, k + 1)
                act.activation(xT[:, k], ps[:, 2 + k % 4], ACT.Copy).then_inc(xT_made_act, 1)
            split_hi(0, 16, None)
            act.wait_ge(start_dve, 8)
            act.activation(rst[:, :], rst[:, :], ACT.Sqrt).then_inc(start_act, 1)
            for u in range(1, U_MIX + AHEAD):
                split_hi(u, 16 * raw_count(u), None)
                if u == 3:
                    act.wait_ge(rb_done, 1)
                    act.activation(rb[:], ps[:, 6], ACT.Copy).then_inc(rb_made, 1)
            for k in range(KT):
                act.wait_ge(ada0_made, 2 + 2 * (k // 4))
                act.wait_ge(xn_made, k + 1)
                act.activation(h_hi[:, k], xn[:, k], ACT.Identity, bias=ada[:, k:k + 1],
                               scale=a_mix[:, k:k + 1]).then_inc(h_hi_made, 1)
                if k >= 2:
                    act.wait_ge(h_lo_made, k - 1)
                act.activation(h_tmp[:, k % 2], xn[:, k], ACT.Identity, bias=ada[:, k:k + 1],
                               scale=a_mix[:, k:k + 1]).then_inc(h_tmp_made, 1)
            split_hi(U_MIX + AHEAD, 16 * raw_count(U_MIX + AHEAD), None)
            act.wait_ge(start_dve, 3)
            act.activation(lbt[:, 1:3].rearrange("p a k -> p (a k)"), lbt[:, 1:3].rearrange("p a k -> p (a k)"),
                           ACT.Exp).then_inc(start_act, 1)
            act.wait_ge(proj_done, 1)
            act.activation(lrT[:, :], ps[0:LOWRANK, B_MISC], ACT.Copy).then_inc(taken_act, 1)

            def exps(g, h, inv):
                s = h % 2
                act.wait_ge(d_made, g * 6 + 2 * h + 2)
                if h == 2:
                    act.wait_ge(o_done, g * 4 + 2)
                act.activation(kp[:, s], d_last[:, s], ACT.Exp, scale=-inv).then_inc(exp_made, 1)
                act.activation(decay[:, h], bcum[:, s, CHUNK - 1::CHUNK], ACT.Exp, scale=inv).then_inc(exp_made, 1)
                act.activation(ks[:, s], d_ref[:, s], ACT.Exp, scale=-inv).then_inc(exp_made, 1)
                act.activation(qs[:, s], d_ref[:, s], ACT.Exp, scale=inv).then_inc(exp_made, 1)
                act.activation(qe[:, s], bcum[:, s], ACT.Exp, scale=inv).then_inc(exp_made, 1)

            def take_kT(g, h, u_free):
                act.wait_ge(turned, g * 3 + h + 1)
                act.wait_ge(u_done, g * 4 + u_free)
                act.activation(kT[:].rearrange("p t c -> p (t c)"), ps[:, MISC_T[h]], ACT.Copy).then_inc(kT_made, 1)

            def take_o(g, w, nw):
                act.wait_ge(o_done, g * 4 + w + 1)
                act.wait_ge(y_made, g * 4 + max(w - 1, 0))
                act.wait_ge(ss_done, g * 3 + w // 2)
                act.activation(sq[:, w % 2], ps[:, B_O + w % 2], ACT.Square).then_inc(sq_made, 1)
                act.activation(oe[:, w % 2], ps[:, B_O + w % 2], ACT.Copy, scale=nw).then_inc(o_taken, 1)

            def root(g, i, bank, dv):
                act.wait_ge(ss_done, g * 3 + i + 1)
                act.wait_ge(normed, g * 4 + (0, 2, 3)[i])
                act.activation(rn[:], ps[:, bank], ACT.Ln, bias=eps_c, scale=SCALE2 / dv).then_inc(ss_taken, 1)
                act.wait_ge(ss_taken, g * 3 + i + 1)
                act.activation(rn[:], rn[:], ACT.Exp, scale=-0.5).then_inc(rn_made, 1)

            act.wait_ge(xT_out, 16)

            def group(g, first):
                for n in range(NU):
                    if n == 0 and not first or n == 1 or n >= 5:
                        split_hi_g(g, n + AHEAD)
                    if n == 4:
                        for m in (6, 7, 8):
                            split_hi_g(g, m)
                    if n in (8, 12, 14):
                        take_kT(g, *{8: (0, 0), 12: (1, 2), 14: (2, 3)}[n])
                    if n == 10:
                        exps(g, 1, 1.0)
                    if n == 11:
                        exps(g, 2, 1.0)
                    act.wait_ge(proj_done, g * NU + n + 2)
                    bank = ps[:, V_BANKS[n] if first and n < 4 else B_PROJ + (U_MIX + n) % 2]
                    if n < 4:
                        act.activation(v[:, n], bank, ACT.Copy).then_inc(taken_act, 1)
                    if n == 4:
                        act.wait_ge(qq_made, g * 6)
                        act.activation(qry[:, 1], bank, ACT.Copy).then_inc(taken_act, 1)
                    if n == 5:
                        act.activation(key[:, 1], bank, ACT.Copy).then_inc(taken_act, 1)
                    if n in (6, 7):
                        i = n - 6
                        if i == 0:
                            act.wait_ge(la_made, g + 1)
                            act.wait_ge(scan_made, g * 3 + 1)
                        else:
                            act.wait_ge(kk_made, g * 6 + 2)
                        act.activation(lg[:, i], bank, ACT.Sigmoid).then_inc(sig_made, 1)
                        act.activation(key[:, i], bank, ACT.Sigmoid, scale=-1.0).then_inc(taken_act, 1)
                    if n in (8, 9):
                        i = n - 8
                        act.wait_ge(qq_made, g * 6 + 2)
                        act.activation(qry[:, i], bank, ACT.Sigmoid).then_inc(sig_made, 1)
                    if n in (10, 12, 14, 16):
                        w = (n - 10) // 2
                        act.wait_ge(merged_made, g * 2)
                        act.activation(gate[:, w], bank, ACT.Sigmoid).then_inc(sig_made, 1)
                    if n in (11, 13, 15, 17):
                        w = (n - 11) // 2
                        act.wait_ge(gated, g * 4 + w)
                        act.activation(gmul[:], bank, ACT.Sigmoid).then_inc(taken_act, 1)
                    if n == 3:
                        act.wait_ge(z_made, g + 1)
                        act.activation(lg[:, 1], lg[:, 0], ACT.Abs).then_inc(soft_step, 1)
                        act.wait_ge(soft_step, g * 3 + 1)
                        act.activation(lg[:, 1], lg[:, 1], ACT.Exp, scale=-1.0).then_inc(soft_step, 1)
                        act.wait_ge(soft_step, g * 3 + 2)
                        act.activation(lg[:, 1], lg[:, 1], ACT.Ln, bias=one_c).then_inc(soft_step, 1)
                    if n == 5:
                        exps(g, 0, 1.0 / LOGIT_NORM)
                    if n == 9:
                        for i in range(2):
                            act.wait_ge(sig_made, g * 8 + i + 1)
                            act.activation(lg[:, i], lg[:, i], ACT.Ln, bias=lb[:, bass.ds(g * 2 + i, 1)],
                                           scale=omlb[:, bass.ds(g * 2 + i, 1)]).then_inc(ln_made, 1)
                    if n == 10:
                        take_o(g, 0, gnw[:, 0:1])
                    if n == 11:
                        take_o(g, 1, gnw[:, 1:2])
                    if n == 12:
                        root(g, 0, MISC_SS[0], GLA_DV)
                    if n == 14:
                        take_o(g, 2, hnw)
                    if n == 16:
                        take_o(g, 3, hnw)
                        root(g, 1, MISC_SS[1], HGRN_DV)
                    if n == 0 and not first:
                        root(g - 1, 2, MISC_SS[2], HGRN_DV)

            group(0, True)
            with act.Fori(1, GROUPS) as g:
                group(g, False)

            act.wait_ge(proj_done, U_OUT)
            def split_u(u):
                split_hi(u, 16 * raw_count(u), u - 5)

            for k in range(KT):
                if k == 6:
                    root(GROUPS - 1, 2, MISC_SS[2], HGRN_DV)
                    split_u(U_OUT + 4)
                    split_u(U_OUT + 5)
                act.wait_ge(merged_made, k + 1)
                act.activation(h_hi[:, k], merged[:, k], ACT.Copy).then_inc(m_hi_made, 1)
            act.activation(cols[:, 62:63], one_c, ACT.Ln).then_inc(start_act, 1)
            for j in range(KT):
                act.wait_ge(hres_made, j + 1)
                if j >= 3:
                    act.wait_ge(sq2_summed, j - 2)
                act.activation(n_tmp[:, j % 2] if j else rn2[:], hres[:, j], ACT.Square).then_inc(sq2_made, 1)
                act.wait_ge(a_ffn_made, 1)
                act.activation(prod[:, KT + j], hres[:, j], ACT.Copy, scale=a_ffn[:, j:j + 1]).then_inc(ha_made, 1)
                if 1 <= j < KT - 1:
                    split_u(U_OUT + j + 5)
            act.wait_ge(ss2_done, 1)
            act.activation(rn2[:], ps[:, B_MISC], ACT.Ln, bias=eps_c, scale=1.0 / D).then_inc(rn2_step, 1)
            act.wait_ge(rn2_step, 1)
            act.activation(rn2[:], rn2[:], ACT.Exp, scale=-0.5).then_inc(rn2_step, 1)
            for k in range(KT):
                act.wait_ge(n_made, k + 1)
                act.activation(h_hi[:, k], n_tmp[:, k % 2], ACT.Identity, bias=ada[:, 24 + k:25 + k]
                               ).then_inc(n_hi_made, 1)
            split_u(U_UP + 4)
            split_u(U_UP + 5)

            def conv_unit(r, m):
                u = U_UP + m
                if not (isinstance(r, int) and m < 2):
                    split_hi(u + AHEAD, (r * 2 + raw_count(u + AHEAD)) * 16, r * 6 + u + AHEAD - 5)
                ch = r * 3 + (m // 2) + (m % 2) * FT
                act.wait_ge(proj_done, r * 6 + u + 1)
                act.activation(conv[:, m], ps[:, m], ACT.Identity, bias=vecs[:, bass.ds(ch + V_CONVB, 1)],
                               scale=vecs[:, bass.ds(ch + V_TAP2, 1)]).then_inc(conv_a, 1)

            def silu_unit(r, m):
                act.wait_ge(conv_made, r * 6 + m + 1)
                act.activation(conv[:, m], conv[:, m], ACT.Silu).then_inc(gate_made, 1)

            for m in range(6):
                conv_unit(0, m)
                if m % 2:
                    silu_unit(0, m - 1)
            with act.Fori(1, 7) as r:
                for m in range(6):
                    act.wait_ge(prod_made, r * 3 + m // 2 - 2)
                    conv_unit(r, m)
                    if m % 2:
                        silu_unit(r, m - 1)
            def prod_hi(r, f, free, dst=None):
                act.wait_ge(prod_made, r * 6 + f + 1)
                act.wait_ge(proj_done, free)
                act.activation(dst if dst is not None else h_hi[:, f % 6], prod[:, bass.ds(r * 6 + f, 1), :].rearrange("p a t -> p (a t)"),
                               ACT.Copy).then_inc(p_hi_made, 1)

            act.wait_ge(prod_made, 19)
            for m in range(2):
                u = U_UP + 42 + m
                split_hi(u + AHEAD, 16 * raw_count(u + AHEAD), u + AHEAD - 5)
                if m == 1:
                    prod_hi(0, 0, 0, p0_hi[:])
                act.wait_ge(proj_done, u + 1)
                ch = 21 + m * FT
                act.activation(conv[:, m], ps[:, m], ACT.Identity, bias=vecs[:, V_CONVB + ch:V_CONVB + ch + 1],
                               scale=vecs[:, V_TAP2 + ch:V_TAP2 + ch + 1]).then_inc(conv_a, 1)
            act.wait_ge(conv_made, 43)
            act.activation(conv[:, 0], conv[:, 0], ACT.Silu).then_inc(gate_made, 1)

            for f in range(1, AHEAD):
                prod_hi(0, f, U_DOWN)
            with act.Fori(0, 3) as r:
                for m in range(6):
                    u = U_DOWN + m + AHEAD
                    split_hi(u, (r * 2 + raw_count(u)) * 16, r * 6 + u - 5)
                    prod_hi(r, m + AHEAD, r * 6 + max(u - 5, U_DOWN))
            act.activation(cols[:, 62:63], one_c, ACT.Sqrt).then_inc(start_act, 1)
            for t in range(TT):
                for half in range(2):
                    act.wait_ge(fin_step, 4 * t + 2 * half + 2)
                    act.activation(prod[:, half], hres_tok[:, t, half * T:(half + 1) * T], ACT.Square,
                                   accum_out=fss[:, 2 * t + half:2 * t + half + 1]).then_inc(fsq_made, 1)
                act.wait_ge(frs_made, 2 * t + 2)
                act.activation(frs[:, t:t + 1], frs[:, t:t + 1], ACT.Sqrt, scale=float(D)).then_inc(fsq_made, 1)
                if t < TT - 1:
                    act.wait_ge(fsq_made, 3 * t + 3)
                    act.activation(hres_tok[:, t], hres_tok[:, t], ACT.Copy, scale=frs[:, t:t + 1]
                                   ).then_inc(fin_scaled, 1)

        @block.vector
        def _(dve):
            def split_lo(u, count):
                dve.wait_ge(hi_made, count)
                dve.tensor_tensor(w_lo[:, slot(u)].rearrange("p k c -> p (k c)"),
                                  raw[:, raw_slot(u)].rearrange("p k c -> p (k c)"),
                                  w_hi[:, slot(u)].rearrange("p k c -> p (k c)").bitcast(F32),
                                  ALU.subtract).then_inc(lo_made, 1)

            dve.memset(rows[:], 0.0).then_inc(rows_zero, 1)
            dve.memset(cols[:, 0:1], EPS).then_inc(cols_made, 1)
            dve.memset(cols[:, 1:2], 1.0).then_inc(cols_made, 1)
            dve.memset(qscale, float(SCALE2) ** 0.5).then_inc(cols_made, 1)
            for i in range(3):
                dve.wait_ge(vecs_turned, 3)
                dve.tensor_copy(vecs[:, i * P:(i + 1) * P], ps[:, 0, i * P:(i + 1) * P]).then_inc(vecs_made, 1)
            dve.wait_ge(vecs_made, 3)
            l0, l1 = vecs[:, V_LB:V_LB + 8], vecs[:, V_LB + 8:V_LB + 16]
            dve.tensor_tensor(lbt[:, 0], l0, l1, ALU.max).then_inc(start_dve, 1)
            dve.wait_ge(start_dve, 1)
            dve.tensor_tensor(lbt[:, 1], l0, lbt[:, 0], ALU.subtract).then_inc(start_dve, 1)
            dve.tensor_tensor(lbt[:, 2], l1, lbt[:, 0], ALU.subtract).then_inc(start_dve, 1)
            dve.wait_ge(cols_made, 3)
            dve.tensor_scalar(gnw, vecs[:, V_GNW:V_GNW + 2], qscale, None, ALU.mult).then_inc(start_dve, 1)
            dve.tensor_scalar(hnw, vecs[:, V_HNW:V_HNW + 1], qscale, None, ALU.mult).then_inc(start_dve, 1)
            dve.wait_ge(start_act, 2)
            dve.tensor_tensor(c_act, c_act, vecs[:, V_C:V_C + 8], ALU.mult).then_inc(start_dve, 1)
            dve.wait_ge(start_dve, 6)

            def ada0_rows(q, k):
                dve.wait_ge(ada0_in[k], 16 * (q + 1))
                if k == 0:
                    ins = dve.tensor_scalar(ada_acc0[:, q], ada_w0[:, 0], c_act[:, 0:1], None, ALU.mult)
                else:
                    dve.wait_ge(ada0_used, q * KT + k)
                    ins = dve.scalar_tensor_tensor(out=ada_acc0[:, q], in0=ada_w0[:, k], scalar=c_act[:, k:k + 1],
                                                   in1=ada_acc0[:, q], op0=ALU.mult, op1=ALU.add)
                ins.then_inc(ada0_used, 1)

            def ada0_finish(q):
                def half(ap):
                    return ap.rearrange("p (a b) -> p a b", b=8)[:, :, 4 * q:4 * q + 4]
                dve.wait_ge(ada0_summed, q + 1)
                dve.tensor_tensor(half(ada[:, 0:16]), ps[:, 7, 8 * q:8 * q + 8].rearrange("p (a b) -> p a b", b=4),
                                  half(vecs[:, V_BADA:V_BADA + 16]), ALU.add).then_inc(ada0_made, 1)
                dve.wait_ge(ada0_made, 2 * q + 1)
                dve.scalar_tensor_tensor(out=a_mix[:, 4 * q:4 * q + 4], in0=ada[:, 8 + 4 * q:12 + 4 * q], scalar=1.0,
                                         in1=vecs[:, V_NMIX + 4 * q:V_NMIX + 4 * q + 4],
                                         op0=ALU.add, op1=ALU.mult).then_inc(ada0_made, 1)
                dve.wait_ge(ada0_made, 2 * q + 2)

            def h_rest(k):
                dve.wait_ge(h_tmp_made, k + 1)
                dve.tensor_tensor(h_lo[:, k], h_tmp[:, k % 2], h_hi[:, k].bitcast(F32), ALU.subtract
                                  ).then_inc(h_lo_made, 1)

            for k in range(KT):
                ada0_rows(0, k)
                if k < 4:
                    j = 2 * k + 1
                    dve.wait_ge(x_turned, j + 1)
                    dve.tensor_copy(xT[:, j], ps[:, 2 + j % 4]).then_inc(xT_made_dve, 1)
                if k == 3:
                    dve.wait_ge(start_act, 6)
                    dve.tensor_scalar(rst, ssq, 1.0 / D, EPS, ALU.mult, ALU.add).then_inc(start_dve, 1)
                    dve.wait_ge(start_dve, 7)
                    dve.reciprocal(rst, rst).then_inc(start_dve, 1)
                if k in (3, 4, 5):
                    split_lo(k - 3, k - 2)
                if k == 5:
                    dve.wait_ge(start_act, 7)
                    for t in range(TT):
                        dve.tensor_scalar(h_tmp[:, 1, t * P:(t + 1) * P], ident[:], rst[:, t:t + 1], None,
                                          ALU.mult).then_inc(rdiag_made, 1)
            split_lo(3, 4)
            split_lo(4, 5)
            ada0_finish(0)
            rows_after = (1, 2, 2, 3)
            done = 0
            for k in range(4):
                h_rest(k)
                for _ in range(rows_after[k]):
                    ada0_rows(1, done)
                    done += 1
            ada0_finish(1)
            for k in range(4, KT):
                h_rest(k)
            split_lo(U_MIX + AHEAD, U_MIX + AHEAD + 1)
            dve.wait_ge(start_act, 8)
            dve.tensor_tensor(lbt[:, 3], lbt[:, 1], lbt[:, 2], ALU.add).then_inc(start_dve, 1)
            dve.wait_ge(start_dve, 9)
            dve.reciprocal(lbt[:, 4], lbt[:, 3]).then_inc(start_dve, 1)
            dve.wait_ge(start_dve, 10)
            dve.tensor_tensor(lb, lbt[:, 1], lbt[:, 4], ALU.mult).then_inc(start_dve, 1)
            dve.wait_ge(start_dve, 11)
            dve.tensor_scalar(omlb, lb, -1.0, 1.0, ALU.mult, ALU.add).then_inc(start_dve, 1)
            dve.wait_ge(gk2_in, 16)

            def decays(g, h, b):
                b3 = bcum[:, b].rearrange("p (c t) -> p c t", t=CHUNK)
                if h:
                    dve.wait_ge(ln_made, g * 2 + h)
                dve.wait_ge(exp_made, g * 15 + (0, 0, 5)[h])
                src = lg[:, max(h - 1, 0)]
                dve.tensor_tensor_scan(bcum[:, b], scan_mask[:], src, 0.0, ALU.mult, ALU.add).then_inc(scan_made, 1)
                dve.wait_ge(scan_made, g * 3 + h + 1)
                for dst, at in ((d_last, CHUNK - 1), (d_ref, CHUNK // 2 - 1)):
                    dve.tensor_tensor(dst[:, b].rearrange("p (c t) -> p c t", t=CHUNK), b3,
                                      b3[:, :, at:at + 1].to_broadcast([P, NCH, CHUNK]),
                                      ALU.subtract).then_inc(d_made, 1)

            def times_k(g, h):
                s = h % 2
                for i, e in enumerate((kp, ks)):
                    dve.wait_ge(exp_made, g * 15 + 5 * h + (1, 3)[i])
                    if h == 0:
                        ins = dve.tensor_tensor(e[:, s], e[:, s], key[:, 1], ALU.mult)
                    else:
                        ins = dve.scalar_tensor_tensor(out=e[:, s], in0=key[:, h - 1],
                                                       scalar=omlb[:, bass.ds(g * 2 + (h - 1), 1)], in1=e[:, s],
                                                       op0=ALU.mult, op1=ALU.mult)
                    ins.then_inc(kk_made, 1)

            def mask_scores(g, h):
                dve.wait_ge(scored, g * 3 + h + 1)
                dve.wait_ge(o_done, g * 4 + (0, 2, 3)[h])
                dve.memset(cols[:, 63:64], 0.0)
                dve.copy_predicated(sT[:], causal[:].bitcast(U32).unsqueeze(1).to_broadcast([P, TT, P]),
                                    ps[:, MISC_S[h]].rearrange("p (t i) -> p t i", i=P)).then_inc(sT_made, 1)

            def states(g, w, h):
                dve.wait_ge(o_done, g * 4 + w)
                for i in range(NCH - 1):
                    if i == 0:
                        dve.wait_ge(u_done, g * 4 + w + 1)
                    u = ps[:, B_STATE + i % 2, (i // 2) * P:(i // 2 + 1) * P]
                    if i == 0:
                        ins = dve.tensor_copy(state[:, 0], u)
                    else:
                        dve.wait_ge(state_made, g * 28 + 7 * w + i)
                        ins = dve.scalar_tensor_tensor(out=state[:, i], in0=state[:, i - 1],
                                                       scalar=decay[:, h, i:i + 1], in1=u,
                                                       op0=ALU.mult, op1=ALU.add)
                    ins.then_inc(state_made, 1)

            def silu(g, n, buf):
                dve.wait_ge(sig_made, g * 8 + (3, 4, 5, 6, 7, 8)[BY_DVE.index(n)])
                dve.tensor_tensor(buf, ps[:, B_PROJ + (U_MIX + n) % 2], buf, ALU.mult).then_inc(taken_dve, 1)

            def ada_rows(g, m):
                dve.wait_ge(ada_in[m % 2], (g * 4 + m // 2 + 1) * 16)
                if m == 0:
                    dve.wait_ge(ada_summed, g)
                    ins = dve.tensor_scalar(ada_acc[:], ada_w[:, 0], c_act[:, 0:1], None, ALU.mult)
                else:
                    dve.wait_ge(ada_used, g * KT + m)
                    ins = dve.scalar_tensor_tensor(out=ada_acc[:], in0=ada_w[:, m % 2], scalar=c_act[:, m:m + 1],
                                                   in1=ada_acc[:], op0=ALU.mult, op1=ALU.add)
                ins.then_inc(ada_used, 1)

            def norm(g, w, i):
                dve.wait_ge(rn_made, g * 3 + i + 1)
                dve.wait_ge(o_taken, g * 4 + w + 1)
                dve.tensor_tensor(oe[:, w % 2], oe[:, w % 2], rn[:], ALU.mult).then_inc(normed, 1)

            def gla_decays(g):
                dve.wait_ge(z_done, g + 1)
                dve.tensor_scalar(lg[:, 0], ps[:, MISC_Z], vecs[:, bass.ds(g + V_BGK, 1)], None, ALU.add
                                  ).then_inc(z_made, 1)
                dve.wait_ge(soft_step, g * 3 + 3)
                dve.scalar_tensor_tensor(out=lg[:, 0], in0=lg[:, 0], scalar=0.0, in1=lg[:, 1],
                                         op0=ALU.min, op1=ALU.subtract).then_inc(la_made, 1)
                dve.wait_ge(la_made, g + 1)
                decays(g, 0, 0)

            def group(g, first):
                if not first:
                    dve.wait_ge(z_done, g)
                dve.tensor_copy(gk2[0:LOWRANK, 0:P], gk2[32:32 + LOWRANK, bass.ds(g * P, P)]).then_inc(gk2_made, 1)
                if first:
                    dve.wait_ge(xT_out, 16)
                    dve.wait_ge(mask_made, 6)
                for n in range(NU):
                    ms = [n + AHEAD] if (n == 0 and not first or n == 1 or n >= 5) else ([6, 7, 8] if n == 4 else [])
                    for m in ms:
                        split_lo(U_MIX + m, g * NU + U_MIX + m + 1)
                    if n == 0 and not first:
                        norm(g - 1, 3, 2)
                    if first and n == 1:
                        gla_decays(g)
                    if first and 5 <= n < 13:
                        ada_rows(g, n - 5)
                    if not first and 1 <= n < 9:
                        ada_rows(g, n - 1)
                    if not first and n == 3:
                        gla_decays(g)
                    if n == 5:
                        dve.wait_ge(taken_act, g * N_ACT + taken_counts(5)[1] + 1)
                        times_k(g, 0)
                    if n == 7:
                        mask_scores(g, 0)
                    if n == 8:
                        silu(g, 8, qry[:, 0])
                        states(g, 0, 0)
                    if n == 9:
                        silu(g, 9, qry[:, 1])
                        decays(g, 1, 1)
                        states(g, 1, 0)
                        decays(g, 2, 0)
                    if n == 10:
                        times_k(g, 1)
                        silu(g, 10, gate[:, 0])
                    if n == 11:
                        times_k(g, 2)
                        mask_scores(g, 1)
                    if n == 12:
                        silu(g, 12, gate[:, 1])
                        states(g, 2, 1)
                    if n == 13:
                        norm(g, 0, 0)
                        norm(g, 1, 0)
                    if n == 14:
                        mask_scores(g, 2)
                        silu(g, 14, gate[:, 2])
                        states(g, 3, 2)
                    if n == 16:
                        silu(g, 16, gate[:, 3])
                        norm(g, 2, 1)
                    if n == 17:
                        dve.wait_ge(ada_summed, g + 1)
                        dve.tensor_tensor(ada[:, bass.ds(g * 8 + 16, 8)], ps[:, B_STATE + 1, 3 * P:3 * P + 8],
                                          vecs[:, bass.ds(g * 8 + V_BADA + 16, 8)], ALU.add).then_inc(ada_made, 1)

            group(0, True)
            with dve.Fori(1, GROUPS) as g:
                group(g, False)

            for k in range(KT):
                if k == 6:
                    norm(GROUPS - 1, 3, 2)
                    split_lo(U_OUT + 4, U_OUT + 5)
                    split_lo(U_OUT + 5, U_OUT + 6)
                dve.wait_ge(m_hi_made, k + 1)
                dve.tensor_tensor(h_lo[:, k], merged[:, k], h_hi[:, k].bitcast(F32), ALU.subtract).then_inc(m_lo_made, 1)
            dve.wait_ge(ada_made, GROUPS)
            dve.scalar_tensor_tensor(out=a_ffn, in0=ada[:, 32:40], scalar=1.0, in1=vecs[:, V_NFFN:V_NFFN + 8],
                                     op0=ALU.add, op1=ALU.mult).then_inc(a_ffn_made, 1)
            dve.wait_ge(const_made, 3)
            dve.wait_ge(m_lo_made, KT)
            for j in range(KT):
                dve.tensor_scalar(prod[:, j // 4, (j % 4) * P:(j % 4 + 1) * P], ident[:], ada[:, 40 + j:41 + j], None,
                                  ALU.mult).then_inc(diag_made, 1)
            dve.wait_ge(xT_back, 16)
            def take_token_major(t):
                dve.wait_ge(ht_done, t + 1)
                dve.tensor_copy(hres_tok[:, t].rearrange("p (a b) -> p a b", a=2),
                                ps[:, B_O - 2 * (t % 2):B_O - 2 * (t % 2) + 2]).then_inc(ht_made, 1)

            for j in range(KT):
                dve.wait_ge(proj_done, U_OUT + max(j, 3) + 1)
                dve.scalar_tensor_tensor(out=hres[:, j], in0=ps[:, OUT_BANKS[j % 4]],
                                         scalar=ada[:, 16 + j:17 + j], in1=hres[:, j],
                                         op0=ALU.mult, op1=ALU.add).then_inc(hres_made, 1)
                if j >= 2:
                    dve.wait_ge(sq2_made, j)
                    if j >= 3:
                        dve.wait_ge(sq2_summed, j - 2)
                    dve.tensor_tensor(rn2[:], rn2[:], n_tmp[:, (j - 1) % 2], ALU.add).then_inc(sq2_summed, 1)
                    split_lo(U_OUT + j + 4, U_OUT + j + 5)
                if j == 5:
                    dve.wait_ge(gf_done, 1)
                    dve.tensor_copy(gf_b[:].rearrange("p (a b) -> p a b", a=2), ps[:, B_O:B_O + 2]).then_inc(gf_made, 1)
            dve.wait_ge(rn2_step, 2)
            dve.wait_ge(ha_made, KT)

            def n_scaled(k):
                if k >= 2:
                    dve.wait_ge(n_lo_made, k - 1)
                dve.tensor_tensor(n_tmp[:, k % 2], prod[:, KT + k], rn2[:], ALU.mult).then_inc(n_made, 1)

            n_scaled(0)
            for k in range(KT):
                if k < KT - 1:
                    n_scaled(k + 1)
                dve.wait_ge(n_hi_made, k + 1)
                dve.scalar_tensor_tensor(out=h_lo[:, k], in0=n_tmp[:, k % 2], scalar=ada[:, 24 + k:25 + k],
                                         in1=h_hi[:, k].bitcast(F32), op0=ALU.add, op1=ALU.subtract
                                         ).then_inc(n_lo_made, 1)
                if k in TAKE_AFTER:
                    take_token_major(TAKE_AFTER.index(k))
            split_lo(U_UP + 4, U_UP + 5)
            split_lo(U_UP + 5, U_UP + 6)

            def taps(r, m, b, end):
                ch = r * 3 + (m // 2) + (m % 2) * FT if end is None else end + (m % 2) * FT
                dve.wait_ge(conv_a, r * 6 + b + 1)
                dve.scalar_tensor_tensor(out=conv[:, m, 1:T], in0=ps[:, m, 0:T - 1],
                                         scalar=vecs[:, bass.ds(ch + V_TAP1, 1)], in1=conv[:, m, 1:T],
                                         op0=ALU.mult, op1=ALU.add).then_inc(conv_b_, 1)
                dve.wait_ge(conv_b_, r * 6 + b + 1)
                dve.scalar_tensor_tensor(out=conv[:, m, 2:T], in0=ps[:, m, 0:T - 2],
                                         scalar=vecs[:, bass.ds(ch + V_TAP0, 1)], in1=conv[:, m, 2:T],
                                         op0=ALU.mult, op1=ALU.add).then_inc(conv_made, 1)

            def up_round(r, first):
                for m in range(6):
                    u = U_UP + m + AHEAD
                    if not (first and m < 2):
                        split_lo(u, r * 6 + u + 1)
                    taps(r, m, m, None)

            up_round(0, True)
            with dve.Fori(1, 7) as r:
                up_round(r, False)

            def prod_lo(r, f, lo=None, hi=None):
                dve.wait_ge(p_hi_made, r * 6 + f + 1)
                if lo is None:
                    lo, hi = h_lo[:, f % 6], h_hi[:, f % 6]
                dve.tensor_tensor(lo, prod[:, bass.ds(r * 6 + f, 1), :].rearrange("p a t -> p (a t)"),
                                  hi.bitcast(F32), ALU.subtract).then_inc(p_lo_made, 1)

            for m in range(2):
                u = U_UP + 42 + m + AHEAD
                split_lo(u, u + 1)
                if m == 1:
                    prod_lo(0, 0, p0_lo[:], p0_hi[:])
                taps(0, m, 42 + m, 21)
            for f in range(1, AHEAD):
                prod_lo(0, f)
            with dve.Fori(0, 3) as r:
                for m in range(6):
                    u = U_DOWN + m + AHEAD
                    split_lo(u, r * 6 + u + 1)
                    prod_lo(r, m + AHEAD)
            dve.wait_ge(gf_made, 1)
            dve.wait_ge(fw_in, 16)
            dve.wait_ge(ht_made, TT)
            for t in range(TT):
                for half in range(2):
                    d = slice(half * T, (half + 1) * T)
                    y = prod[:, 2 + half]
                    i = 4 * t + 2 * half
                    dve.wait_ge(y_done, 2 * t + half + 1)
                    dve.tensor_tensor(y, ps[:, 2 * t + half], gf_b[:, d], ALU.mult).then_inc(fin_step, 1)
                    dve.wait_ge(fin_step, i + 1)
                    dve.tensor_tensor(hres_tok[:, t, d], hres_tok[:, t, d], y, ALU.add).then_inc(fin_step, 1)
                dve.wait_ge(fsq_made, 3 * t + 2)
                dve.tensor_scalar(frs[:, t:t + 1], fss[:, 2 * t:2 * t + 1], fss[:, 2 * t + 1:2 * t + 2], EPS * D,
                                  ALU.add, ALU.add).then_inc(frs_made, 1)
                dve.wait_ge(frs_made, 2 * t + 1)
                dve.reciprocal(frs[:, t:t + 1], frs[:, t:t + 1]).then_inc(frs_made, 1)
            dve.wait_ge(fsq_made, 3 * TT)
            for half in range(2):
                d = slice(half * T, (half + 1) * T)
                dve.scalar_tensor_tensor(out=hres_tok[:, t, d], in0=hres_tok[:, t, d], scalar=frs[:, t:t + 1],
                                         in1=fw_b[:, d], op0=ALU.mult, op1=ALU.mult).then_inc(fin_last, 1)

        @block.tensor
        def _(pe):
            def three(dst, pairs, start=True, stop=True):
                n = len(pairs)
                for i, ((a_hi, a_lo), (b_hi, b_lo)) in enumerate(pairs):
                    pe.matmul(dst, a_hi, b_hi, start=start and i == 0, stop=False)
                    pe.matmul(dst, a_hi, b_lo, start=False, stop=False)
                    last = pe.matmul(dst, a_lo, b_hi, start=False, stop=stop and i == n - 1)
                return last

            def unit(u, bank):
                s = slot(u)
                return three(ps[:, bank], [((w_hi[:, s, k], w_lo[:, s, k]), (h_hi[:, k], h_lo[:, k]))
                                           for k in range(KT)])

            pe.wait_ge(rows_in, 16 * 11)
            pe.wait_ge(const_made, 3)
            for i in range(3):
                pe.transpose(ps[:, 0, i * P:(i + 1) * P], rows[:, i], ident[:]).then_inc(vecs_turned, 1)
            pe.wait_ge(x_in, 16)
            for k in range(KT):
                if k >= 4:
                    pe.wait_ge(xT_made_dve if k % 2 else xT_made_act, (k - 4) // 2 + 1)
                for t in range(TT):
                    last = pe.transpose(ps[:, 2 + k % 4, t * P:(t + 1) * P], x_tok[:, t, k * P:(k + 1) * P], ident[:])
                last.then_inc(x_turned, 1)
            pe.wait_ge(rdiag_made, TT)
            for t in range(TT):
                last = pe.matmul(ps[:, 6, t * P:(t + 1) * P], ones[:], h_tmp[:, 1, t * P:(t + 1) * P],
                                 start=True, stop=True)
            last.then_inc(rb_done, 1)

            def ada0_sums(q):
                pe.wait_ge(ada0_used, KT * (q + 1))
                for m in range(8):
                    last = pe.matmul(ps[:, 7, 8 * q + m:8 * q + m + 1], ada_acc0[:, q, m * P:(m + 1) * P],
                                     ones[:, 0:1], start=True, stop=True)
                last.then_inc(ada0_summed, 1)

            ada0_sums(0)
            pe.wait_ge(vecs_made, 3)
            pe.wait_ge(lo_made, U_MIX + AHEAD)
            pe.wait_ge(xT_made_act, KT // 2)
            pe.wait_ge(xT_made_dve, KT // 2)
            for k in range(KT):
                pe.wait_ge(h_lo_made, k + 1)
                last = three(ps[:, B_MISC], [((w_hi[:, slot(0), k], w_lo[:, slot(0), k]), (h_hi[:, k], h_lo[:, k]))],
                             start=k == 0, stop=k == KT - 1)
                if k == KT - 1:
                    last.then_inc(proj_done, 1)
                for t in range(TT):
                    if k == 3 and t == 1:
                        ada0_sums(1)
                    tok = slice(t * P, (t + 1) * P)
                    last = three(ps[:, V_BANKS[t]].rearrange("p (a b) -> p a b", b=P),
                                 [((h_hi[:, k, tok], h_lo[:, k, tok]), (w_hi[:, 0:4, k], w_lo[:, 0:4, k]))],
                                 start=k == 0, stop=k == KT - 1)
                    if k == KT - 1:
                        last.then_inc(proj_done, 1)

            def turn(g, h):
                pe.wait_ge(kk_made, g * 6 + 2 * h + 1)
                for t in range(TT):
                    last = pe.transpose(ps[:, MISC_T[h], t * P:(t + 1) * P], kp[:, h % 2, t * P:(t + 1) * P], ident[:])
                last.then_inc(turned, 1)

            def score(g, h):
                pe.wait_ge(kk_made, g * 6 + 2 * h + 2)
                pe.wait_ge(qq_made, g * 6 + 2 * h + 1)
                half = CHUNK // 2
                for t in range(TT):
                    for j in range(0, P, half):
                        i = slice(t * P + j, t * P + (j // CHUNK + 1) * CHUNK)
                        last = pe.matmul(ps[j:j + half, MISC_S[h], i], ks[:, h % 2, t * P + j:t * P + j + half],
                                         qs[:, h % 2, i], start=True, stop=True)
                last.then_inc(scored, 1)

            def chunk_states(g, w, h):
                pe.wait_ge(kT_made, g * 3 + h + 1)
                pe.wait_ge(state_made, g * 28 + 7 * w)
                for i in range(NCH - 1):
                    if w == 0 and i == 1:
                        pe.wait_ge(ada_made, g)
                    rows_ = slice(CHUNK * (i % 2), CHUNK * (i % 2) + CHUNK)
                    last = pe.matmul(ps[:, B_STATE + i % 2, (i // 2) * P:(i // 2 + 1) * P], kT[rows_, i // 2],
                                     v[rows_, i // 2, w * P:(w + 1) * P], start=True, stop=True)
                last.then_inc(u_done, 1)

            def outputs(g, w, h):
                pe.wait_ge(sT_made, g * 3 + h + 1)
                pe.wait_ge(qq_made, g * 6 + 2 * h + 2)
                pe.wait_ge(o_taken, g * 4 + max(w - 1, 0))
                for t in range(TT):
                    o = ps[:, B_O + w % 2, t * P:(t + 1) * P]
                    pe.matmul(o, v[:, t, w * P:(w + 1) * P], sT[:, t], start=True, stop=False)
                    for i in (2 * t, 2 * t + 1):
                        if i:
                            pe.wait_ge(state_made, g * 28 + 7 * w + i)
                            last = pe.matmul(o[:, (i % 2) * CHUNK:(i % 2 + 1) * CHUNK], state[:, i - 1],
                                             qe[:, h % 2, i * CHUNK:(i + 1) * CHUNK], start=False, stop=i % 2 == 1)
                last.then_inc(o_done, 1)

            def square_sums(g, i, w):
                if i == 0:
                    pe.wait_ge(sq_summed, g + 1)
                else:
                    pe.wait_ge(sq_made, g * 4 + w + 1)
                pe.matmul(ps[:, MISC_SS[i]], ones[:], sq[:, w % 2], start=True, stop=True).then_inc(ss_done, 1)

            def low_rank(g):
                pe.wait_ge(gk2_made, g + 1)
                pe.wait_ge(taken_act, g * N_ACT + 1)
                if not isinstance(g, int):
                    pe.wait_ge(ss_taken, g * 3)
                pe.matmul(ps[:, MISC_Z], gk2[0:LOWRANK, 0:P], lrT[:], start=True, stop=True).then_inc(z_done, 1)

            def group(g, first):
                for n in range(NU):
                    u = U_MIX + n
                    if n == 0 and not first:
                        pe.wait_ge(lo_made, g * NU + U_MIX + 4)
                    elif n >= 4:
                        pe.wait_ge(lo_made, g * NU + u + 1)
                    if first and n == 4:
                        low_rank(0)
                    if first and n in (4, 5):
                        pe.wait_ge(taken_act, n - 2)
                    elif not (first and n < 4):
                        prod_wait(pe, g, n)
                    bank = B_PROJ + u % 2
                    if first and n < 4:
                        continue
                    if n < 4:
                        tok = slice(n * P, (n + 1) * P)
                        last = three(ps[:, bank].rearrange("p (a b) -> p a b", b=P), [((h_hi[:, k, tok], h_lo[:, k, tok]),
                                                    (w_hi[:, 0:4, k], w_lo[:, 0:4, k])) for k in range(KT)])
                    else:
                        last = unit(u, bank)
                    last.then_inc(proj_done, 1)
                    if n == 2:
                        low_rank(g)
                    if n == 7:
                        pe.wait_ge(z_made, g + 1)
                        turn(g, 0)
                        score(g, 0)
                    if n == 8:
                        chunk_states(g, 0, 0)
                    if n == 9:
                        outputs(g, 0, 0)
                        chunk_states(g, 1, 0)
                    if n == 10:
                        outputs(g, 1, 0)
                    if n == 11:
                        pe.wait_ge(sT_made, g * 3 + 1)
                        turn(g, 1)
                        pe.wait_ge(kT_made, g * 3 + 1)
                        score(g, 1)
                    if n == 12:
                        chunk_states(g, 2, 1)
                        square_sums(g, 0, 0)
                    if n == 13:
                        outputs(g, 2, 1)
                        pe.wait_ge(sT_made, g * 3 + 2)
                        turn(g, 2)
                    if n == 14:
                        pe.wait_ge(ss_taken, g * 3 + 1)
                        score(g, 2)
                        chunk_states(g, 3, 2)
                    if n == 15:
                        outputs(g, 3, 2)
                        pe.wait_ge(kT_made, g * 3 + 3)
                        square_sums(g, 1, 2)
                    if n == 16:
                        pe.wait_ge(ada_used, g * KT + KT)
                        pe.wait_ge(state_made, g * 28 + 28)
                        for m in range(KT):
                            last = pe.matmul(ps[:, B_STATE + 1, 3 * P + m:3 * P + m + 1], ada_acc[:, m * P:(m + 1) * P],
                                             ones[:, 0:1], start=True, stop=True)
                        last.then_inc(ada_summed, 1)
                    if n == 17:
                        pe.wait_ge(sT_made, g * 3 + 3)
                        square_sums(g, 2, 3)

            group(0, True)
            with pe.Fori(1, GROUPS) as g:
                group(g, False)

            def interleaved(u0, banks, ready, between=None):
                pe.wait_ge(lo_made, u0 + 4)
                for k in range(KT):
                    if k in (2, 4) and between:
                        between(k)
                    pe.wait_ge(ready, k + 1)
                    for i, bank in enumerate(banks):
                        s = slot(u0 + i)
                        last = three(ps[:, bank], [((w_hi[:, s, k], w_lo[:, s, k]), (h_hi[:, k], h_lo[:, k]))],
                                     start=k == 0, stop=k == KT - 1)
                        if k == KT - 1:
                            last.then_inc(proj_done, 1)

            pe.wait_ge(taken_act, GROUPS * N_ACT + 1)
            pe.wait_ge(taken_dve, GROUPS * N_DVE)
            pe.wait_ge(ada_made, GROUPS)
            interleaved(U_OUT, OUT_BANKS, m_lo_made)
            for j in range(4, KT):
                pe.wait_ge(lo_made, U_OUT + j + 1)
                pe.wait_ge(hres_made, j - 3)
                unit(U_OUT + j, OUT_BANKS[j % 4]).then_inc(proj_done, 1)
                if j == 4:
                    pe.wait_ge(diag_made, KT)
                    pe.wait_ge(o_taken, 4 * GROUPS)
                    for i in range(KT):
                        last = pe.matmul(ps[:, B_O + i // 4, (i % 4) * P:(i % 4 + 1) * P], ones[:],
                                         prod[:, i // 4, (i % 4) * P:(i % 4 + 1) * P], start=True, stop=True)
                    last.then_inc(gf_done, 1)

            def token_major(t):
                if t == 0:
                    pe.wait_ge(gf_made, 1)
                if t == 1:
                    pe.wait_ge(hres_made, KT)
                if t >= 2:
                    pe.wait_ge(ht_made, t - 1)
                for k in range(KT):
                    last = pe.transpose(ps[:, B_O - 2 * (t % 2) + k // 4, (k % 4) * P:(k % 4 + 1) * P],
                                        hres[:, k, t * P:(t + 1) * P], ident[:])
                last.then_inc(ht_done, 1)

            pe.wait_ge(sq2_summed, KT - 2)
            pe.wait_ge(ss_taken, 3 * GROUPS)
            pe.matmul(ps[:, B_MISC], ones[:], rn2[:], start=True, stop=False)
            pe.wait_ge(sq2_made, KT)
            pe.matmul(ps[:, B_MISC], ones[:], n_tmp[:, (KT - 1) % 2], start=False, stop=True).then_inc(ss2_done, 1)
            for t in range(2):
                token_major(t)

            def up_unit(r, m, b):
                pe.wait_ge(lo_made, r * 6 + U_UP + b + 1)
                return unit(U_UP + m, m)

            pe.wait_ge(rn2_step, 1)
            interleaved(U_UP, range(4), n_lo_made, lambda k: token_major(1 + k // 2))
            pe.wait_ge(ht_made, TT)
            for m in (4, 5):
                up_unit(0, m, m).then_inc(proj_done, 1)
            with pe.Fori(1, 7) as r:
                for m in range(6):
                    pe.wait_ge(conv_made, r * 6 + m - 5)
                    up_unit(r, m, m).then_inc(proj_done, 1)
            for m in range(2):
                pe.wait_ge(conv_made, 42 + m - 5)
                up_unit(0, m, 42 + m).then_inc(proj_done, 1)

            def down(a_hi, a_lo, u, t, half, start=False, stop=False):
                s = slot(u)
                tok = slice(t * P, (t + 1) * P)
                cols_ = slice(4 * half, 4 * half + 4)
                return three(ps[:, 2 * t + half].rearrange("p (a b) -> p a b", b=P),
                             [((a_hi[:, tok], a_lo[:, tok]),
                               (w_hi[:, s, cols_], w_lo[:, s, cols_]))], start=start, stop=stop)

            pe.wait_ge(ht_made, TT)
            pe.wait_ge(lo_made, U_DOWN + 1)
            pe.wait_ge(p_lo_made, 1)
            pe.wait_ge(conv_made, 42)
            for t in (3, 1, 2, 0):
                if t == 0:
                    pe.wait_ge(conv_made, 2 * FT)
                for half in range(2):
                    last = down(p0_hi, p0_lo, U_DOWN, t, half, start=True)
            last.then_inc(proj_done, 1)
            with pe.Fori(0, 3) as r:
                for m in range(1, 7):
                    pe.wait_ge(lo_made, r * 6 + U_DOWN + m + 1)
                    pe.wait_ge(p_lo_made, r * 6 + m + 1)
                    for t in range(TT):
                        for half in range(2):
                            last = down(h_hi[:, m % 6], h_lo[:, m % 6], U_DOWN + m, t, half)
                    last.then_inc(proj_done, 1)
            pe.wait_ge(lo_made, U_END)
            pe.wait_ge(p_lo_made, FT)
            for t in range(TT):
                for half in range(2):
                    for f in range(19, FT):
                        last = down(h_hi[:, f % 6], h_lo[:, f % 6], U_DOWN + f, t, half, stop=f == FT - 1)
                    last.then_inc(y_done, 1)


_INS = ["x", "c", "w_ada", "b_ada", "norm_mix_w", "w_in", "w_gk2", "b_gk2", "gla_norm_w", "hgrn_lb",
        "hgrn_norm_w", "w_out", "norm_ffn_w", "w_up", "conv_w", "conv_b", "w_down", "final_norm_w"]


def kernel(**inputs):
    import numpy as np
    import concourse.bacc as bacc
    from concourse.bass_utils import run_bass_kernel_spmd as run

    nc = bacc.Bacc("TRN2", target_bir_lowering=False, num_devices=1)
    arrays, args = {}, []
    for name in _INS:
        a = np.ascontiguousarray(inputs[name])
        arrays[f"in_{name}_dram"] = a
        args.append(nc.dram_tensor(f"in_{name}_dram", a.shape, mybir.dt.from_np(a.dtype), kind="ExternalInput").ap())
    out = nc.dram_tensor("out_dram", (1, T, D), F32, kind="ExternalOutput").ap()
    build(nc, *args, out)
    r = run(nc, [arrays], core_ids=[0])
    return r.results[0]["out_dram"]
```
